# Optimizing a Trainium2 kernel written in Bass

```python
import math
import jax, jax.numpy as jnp
from jax import lax
import numpy as np

D_MODEL = 1024
BATCH = 1
SEQ = 1024
DEPTH = 2
DEC_BATCH = 1
DEC_SEQ = 256
PAST_LEN = 128

HEAD_DIM = 64
DA_HEADS = 4
DA_VDIM = 2 * HEAD_DIM
SW_Q_HEADS = 8
SW_KV_HEADS = 2
SW_GROUP = SW_Q_HEADS // SW_KV_HEADS
WINDOW = 128
BLOCK = 128
N_EXPERTS = 16
EC_CAPACITY_FACTOR = 2
D_EXPERT = 1024
PLE_DIM = 256
ROPE_THETA = 10000.0
NORM_EPS = 1e-6
MASK_VALUE = -1e30

DA_Q = DA_HEADS * 2 * HEAD_DIM
DA_K = DA_HEADS * 2 * HEAD_DIM
DA_V = DA_HEADS * DA_VDIM
SW_Q = SW_Q_HEADS * HEAD_DIM
SW_K = SW_KV_HEADS * HEAD_DIM
SW_V = SW_KV_HEADS * HEAD_DIM
D_IN_PROJ = DA_Q + DA_K + DA_V + SW_Q + SW_K + SW_V
D_MIX = DA_V + SW_Q
SPLITS = (DA_Q, DA_Q + DA_K, DA_Q + DA_K + DA_V, DA_Q + DA_K + DA_V + SW_Q, DA_Q + DA_K + DA_V + SW_Q + SW_K)

kernel_name = "hymba_diffattn_swa_ec_moe_encoder"

def rms_norm(x, g):
    xf = x.astype(jnp.float32)
    y = xf * lax.rsqrt(jnp.mean(xf * xf, axis=-1, keepdims=True) + NORM_EPS)
    return (y * g.astype(jnp.float32)).astype(x.dtype)

def rope_tables(seq_len):
    pos = jnp.arange(seq_len, dtype=jnp.float32)
    inv = ROPE_THETA ** (-jnp.arange(0, HEAD_DIM, 2, dtype=jnp.float32) / HEAD_DIM)
    ang = pos[:, None] * inv[None, :]
    ang = jnp.concatenate([ang, ang], axis=-1)
    return jnp.cos(ang), jnp.sin(ang)

def apply_rope(x, cos, sin):
    shape = (cos.shape[0],) + (1,) * (x.ndim - 3) + (HEAD_DIM,)
    c = cos.reshape(shape)
    s = sin.reshape(shape)
    xf = x.astype(jnp.float32)
    x1, x2 = jnp.split(xf, 2, axis=-1)
    rot = jnp.concatenate([-x2, x1], axis=-1)
    return (xf * c + rot * s).astype(x.dtype)

def diff_attention(q, k, v, lam):
    B, S, H = q.shape[0], q.shape[1], q.shape[2]
    nb = S // BLOCK
    scale = HEAD_DIM ** -0.5
    qb = jnp.moveaxis(q.reshape(B, nb, BLOCK, H, 2, HEAD_DIM), 1, 0)

    def one_block(qblk):
        s = jnp.einsum('bqhcd,bkhcd->bhcqk', qblk, k).astype(jnp.float32) * scale
        p = jax.nn.softmax(s, axis=-1)
        a = p[:, :, 0] - lam * p[:, :, 1]
        return jnp.einsum('bhqk,bkhe->bqhe', a.astype(v.dtype), v)

    o = lax.map(one_block, qb)
    return jnp.moveaxis(o, 0, 1).reshape(B, S, H, DA_VDIM)

def sliding_window_attention(q, k, v, sink):
    B, S = q.shape[0], q.shape[1]
    nb = S // BLOCK
    scale = HEAD_DIM ** -0.5
    qb = q.reshape(B, nb, BLOCK, SW_KV_HEADS, SW_GROUP, HEAD_DIM)
    pad = ((0, 0), (BLOCK, BLOCK), (0, 0), (0, 0))
    kp = jnp.pad(k, pad).reshape(B, nb + 2, BLOCK, SW_KV_HEADS, HEAD_DIM)
    vp = jnp.pad(v, pad).reshape(B, nb + 2, BLOCK, SW_KV_HEADS, HEAD_DIM)
    kb = jnp.concatenate([kp[:, :-2], kp[:, 1:-1], kp[:, 2:]], axis=2)
    vb = jnp.concatenate([vp[:, :-2], vp[:, 1:-1], vp[:, 2:]], axis=2)
    s = jnp.einsum('bnqhgd,bnkhd->bnhgqk', qb, kb).astype(jnp.float32) * scale
    qi = jnp.arange(BLOCK)
    kj = jnp.arange(3 * BLOCK)
    rel = kj[None, :] - BLOCK - qi[:, None]
    kpos = jnp.arange(nb)[:, None] * BLOCK - BLOCK + kj[None, :]
    mask = (jnp.abs(rel) <= WINDOW)[None, :, :] & ((kpos >= 0) & (kpos < S))[:, None, :]
    s = jnp.where(mask[None, :, None, None], s, MASK_VALUE)
    sink_l = sink.astype(jnp.float32).reshape(SW_KV_HEADS, SW_GROUP)[None, None, :, :, None, None]
    m = jnp.maximum(jnp.max(s, axis=-1, keepdims=True), sink_l)
    e = jnp.exp(s - m)
    pr = e / (jnp.sum(e, axis=-1, keepdims=True) + jnp.exp(sink_l - m))
    o = jnp.einsum('bnhgqk,bnkhd->bnqhgd', pr.astype(v.dtype), vb)
    return o.reshape(B, S, SW_Q)

def ec_moe(h, w_router, w_gate, w_up, w_down):
    B, S, D = h.shape
    hf = h.reshape(B * S, D)
    n_tok = hf.shape[0]
    cap = EC_CAPACITY_FACTOR * n_tok // N_EXPERTS
    aff = jax.nn.softmax((hf @ w_router).astype(jnp.float32), axis=-1)
    vals, idx = lax.top_k(aff.T, cap)
    xe = hf[idx]
    g = jnp.einsum('ecd,edf->ecf', xe, w_gate)
    u = jnp.einsum('ecd,edf->ecf', xe, w_up)
    ye = jnp.einsum('ecf,efd->ecd', jax.nn.silu(g) * u, w_down)
    ye = ye * vals[..., None].astype(ye.dtype)
    out = jnp.zeros_like(hf).at[idx.reshape(-1)].add(ye.reshape(-1, D))
    return out.reshape(B, S, D)

def encoder(x, p, attn_norm, w_in, q_norm_a, k_norm_a, lambda_q1, lambda_k1, lambda_q2, lambda_k2,
            subln_a, q_norm_b, k_norm_b, sink_b, w_out, ffn_norm, w_router, w_gate_e, w_up_e, w_down_e,
            ple_norm, w_ple_gate, w_ple_proj):
    B, S, _ = x.shape
    cos, sin = rope_tables(S)
    for i in range(DEPTH):
        lam_init = 0.8 - 0.6 * math.exp(-0.3 * i)
        h = rms_norm(x, attn_norm[i])
        proj = h @ w_in[i]
        qa, ka, va, qb, kb, vb = jnp.split(proj, SPLITS, axis=-1)
        qa = apply_rope(rms_norm(qa.reshape(B, S, DA_HEADS, 2, HEAD_DIM), q_norm_a[i]), cos, sin)
        ka = apply_rope(rms_norm(ka.reshape(B, S, DA_HEADS, 2, HEAD_DIM), k_norm_a[i]), cos, sin)
        va = va.reshape(B, S, DA_HEADS, DA_VDIM)
        lam = (jnp.exp(jnp.sum(lambda_q1[i].astype(jnp.float32) * lambda_k1[i].astype(jnp.float32)))
               - jnp.exp(jnp.sum(lambda_q2[i].astype(jnp.float32) * lambda_k2[i].astype(jnp.float32)))
               + lam_init)
        oa = diff_attention(qa, ka, va, lam)
        oa = rms_norm(oa, subln_a[i]) * (1.0 - lam_init)
        qb = apply_rope(rms_norm(qb.reshape(B, S, SW_Q_HEADS, HEAD_DIM), q_norm_b[i]), cos, sin)
        kb = apply_rope(rms_norm(kb.reshape(B, S, SW_KV_HEADS, HEAD_DIM), k_norm_b[i]), cos, sin)
        vb = vb.reshape(B, S, SW_KV_HEADS, HEAD_DIM)
        ob = sliding_window_attention(qb, kb, vb, sink_b[i])
        mix = jnp.concatenate([oa.reshape(B, S, DA_V), ob], axis=-1)
        x = x + mix @ w_out[i]
        x = x + ec_moe(rms_norm(x, ffn_norm[i]), w_router[i], w_gate_e[i], w_up_e[i], w_down_e[i])
        gate = jax.nn.sigmoid(rms_norm(x, ple_norm[i]) @ w_ple_gate[i])
        x = x + gate * (p[i] @ w_ple_proj[i])
    return x

def setup_inputs(seed: int = 0) -> dict:
    key = jax.random.key(seed)
    ks = jax.random.split(key, 24)
    f32 = jnp.float32

    def nrm(k, shape, scale):
        return jax.random.normal(k, shape, f32) * scale

    def gain(k, shape):
        return 1.0 + 0.05 * jax.random.normal(k, shape, f32)

    return {
        "x_prompt": nrm(ks[0], (BATCH, SEQ, D_MODEL), 1.0),
        "x_sample": nrm(ks[1], (DEC_BATCH, DEC_SEQ, D_MODEL), 1.0),
        "p_prompt": nrm(ks[2], (DEPTH, BATCH, SEQ, PLE_DIM), 1.0),
        "p_sample": nrm(ks[3], (DEPTH, DEC_BATCH, DEC_SEQ, PLE_DIM), 1.0),
        "attn_norm": gain(ks[4], (DEPTH, D_MODEL)),
        "w_in": nrm(ks[5], (DEPTH, D_MODEL, D_IN_PROJ), D_MODEL ** -0.5),
        "q_norm_a": gain(ks[6], (DEPTH, HEAD_DIM)),
        "k_norm_a": gain(ks[7], (DEPTH, HEAD_DIM)),
        "lambda_q1": nrm(ks[8], (DEPTH, HEAD_DIM), 0.1),
        "lambda_k1": nrm(ks[9], (DEPTH, HEAD_DIM), 0.1),
        "lambda_q2": nrm(ks[10], (DEPTH, HEAD_DIM), 0.1),
        "lambda_k2": nrm(ks[11], (DEPTH, HEAD_DIM), 0.1),
        "subln_a": gain(ks[12], (DEPTH, DA_VDIM)),
        "q_norm_b": gain(ks[13], (DEPTH, HEAD_DIM)),
        "k_norm_b": gain(ks[14], (DEPTH, HEAD_DIM)),
        "sink_b": nrm(ks[15], (DEPTH, SW_Q_HEADS), 0.5),
        "w_out": nrm(ks[16], (DEPTH, D_MIX, D_MODEL), D_MIX ** -0.5),
        "ffn_norm": gain(ks[17], (DEPTH, D_MODEL)),
        "w_router": nrm(ks[18], (DEPTH, D_MODEL, N_EXPERTS), D_MODEL ** -0.5),
        "w_gate_e": nrm(ks[19], (DEPTH, N_EXPERTS, D_MODEL, D_EXPERT), D_MODEL ** -0.5),
        "w_up_e": nrm(ks[20], (DEPTH, N_EXPERTS, D_MODEL, D_EXPERT), D_MODEL ** -0.5),
        "w_down_e": nrm(ks[21], (DEPTH, N_EXPERTS, D_EXPERT, D_MODEL), D_EXPERT ** -0.5),
        "ple_norm": gain(ks[22], (DEPTH, D_MODEL)),
        "w_ple_gate": nrm(jax.random.fold_in(ks[23], 0), (DEPTH, D_MODEL, D_MODEL), D_MODEL ** -0.5),
        "w_ple_proj": nrm(jax.random.fold_in(ks[23], 1), (DEPTH, PLE_DIM, D_MODEL), PLE_DIM ** -0.5),
    }

def reference(x_prompt, x_sample, p_prompt, p_sample, attn_norm, w_in, q_norm_a, k_norm_a,
              lambda_q1, lambda_k1, lambda_q2, lambda_k2, subln_a, q_norm_b, k_norm_b, sink_b,
              w_out, ffn_norm, w_router, w_gate_e, w_up_e, w_down_e, ple_norm, w_ple_gate, w_ple_proj):
    y_prompt = encoder(x_prompt, p_prompt, attn_norm, w_in, q_norm_a, k_norm_a, lambda_q1, lambda_k1,
                       lambda_q2, lambda_k2, subln_a, q_norm_b, k_norm_b, sink_b, w_out, ffn_norm,
                       w_router, w_gate_e, w_up_e, w_down_e, ple_norm, w_ple_gate, w_ple_proj)
    y_sample = encoder(x_sample, p_sample, attn_norm, w_in, q_norm_a, k_norm_a, lambda_q1, lambda_k1,
                       lambda_q2, lambda_k2, subln_a, q_norm_b, k_norm_b, sink_b, w_out, ffn_norm,
                       w_router, w_gate_e, w_up_e, w_down_e, ple_norm, w_ple_gate, w_ple_proj)
    return (y_prompt, y_sample)


_drawn_inputs = setup_inputs


def setup_inputs(seed=0):
    import zlib

    import numpy as np

    out = dict(_drawn_inputs(seed))
    spreads = {}
    factors = {'lambda_q1': 2.774, 'q_norm_b': 6.911, 'k_norm_b': 5.614, 'sink_b': 8.0, 'ple_norm': 4.603}
    for name, (base, spread) in spreads.items():
        noise = np.random.default_rng([zlib.crc32(name.encode()), seed]).standard_normal(out[name].shape)
        drawn = base * np.exp(spread * noise) if base else spread * noise
        out[name] = __import__('jax').numpy.asarray(drawn.astype(out[name].dtype))
    for name, factor in factors.items():
        out[name] = (out[name] * factor).astype(out[name].dtype)
    return out
```

```python
import math
from contextlib import ExitStack, contextmanager

import numpy as np

import concourse.bass as bass
from concourse import mybir

ALU = mybir.AluOpType
ACT = mybir.ActivationFunctionType
AX_X = mybir.AxisListType.X
F32 = mybir.dt.float32
F32R = mybir.dt.float32r
BF16 = mybir.dt.bfloat16
U32 = mybir.dt.uint32

P = 128
D = 1024
KD = D // P
DEPTH = 2
PROMPT, SAMPLE = 1024, 256
ROWS = PROMPT + SAMPLE
TILES = ROWS // P
HD = 64
HALF = HD // 2
DA_HEADS, SW_KV, GROUP = 4, 2, 4
NQK = 13
V_W = 640
D_IN = 2304
E = 16
CAP_P, CAP_S = 2 * PROMPT // E, 2 * SAMPLE // E
SLOTS = CAP_P + CAP_S
PLE = 256
EPS = 1e-6
SCALE = HD ** -0.5
MASKED = -1e30
BANK = 512


class Chain:

    def __init__(self, eng, sem, tile, per):
        self.eng, self.sem, self.base, self.per, self.n = eng, sem, tile * per, per, 0

    def link(self, ins):
        ins.then_inc(self.sem, 1)
        self.n += 1
        self.eng.wait_ge(self.sem, self.base + self.n)

    def close(self):
        assert self.n == self.per, (self.sem.name, self.n)


def paired(eng, count, lag, step):
    head = lag + lag % 2
    for i in range(head):
        step(i, i % 2, lambda k, i=i: 0 <= i - k < count, i // 2)
    with eng.Fori(head // 2, count // 2) as j:
        for b in range(2):
            step(j * 2 + b, b, lambda k: True, j)
    for i in range(count, count + lag):
        step(i, i % 2, lambda k, i=i: 0 <= i - k < count, i // 2)


def warm(i):
    return not isinstance(i, int) or i >= 2


def split_matmul(pe, out, a, b, first=True, last=True):
    pe.matmul(out, a[0], b[0], start=first, stop=False)
    pe.matmul(out, a[0], b[1], start=False, stop=False)
    return pe.matmul(out, a[1], b[0], start=False, stop=last)


def over(ap, count):
    w = ap.shape[-1]
    return ap.rearrange("p (a w) -> p a w", a=1).to_broadcast([ap.shape[0], count, w])


def along(ap, width):
    n = ap.shape[-1]
    return ap.rearrange("p (n a) -> p n a", a=1).to_broadcast([ap.shape[0], n, width])


def stage_project(nc, sem, layer, io):
    CH = 256
    NP = D_IN // CH
    CHUNKS = [(0, 8, 0, 0, None), (512, 8, 1, 4, None), (1536, 8, 2, 8, None), (2048, 2, 3, 12, 512),
              (1024, 0, None, None, 0)]
    NCH = len(CHUNKS)
    SPLIT_BY = (2, 4, 6, 7, NP)
    pieces = [c // CH + j for c, *_ in CHUNKS for j in range(2 if c != 2048 else 1)]
    with ExitStack() as ctx:
        def sb(name, shape, dt=F32):
            return ctx.enter_context(nc.sbuf_tensor(name, shape, dt))

        w_raw = sb("p_w_raw", [P, 2, KD, CH])
        w_hi = sb("p_w_hi", [P, KD, D_IN], F32R)
        w_lo = sb("p_w_lo", [P, KD, D_IN], F32R)
        x_in = sb("p_x", [P, 2, D])
        gain_x = sb("p_gain_x", [P, D])
        gains = sb("p_gains", [P, 4, HD])
        trig = sb("p_trig", [P, 2, 2, HD])
        cosg = sb("p_cosg", [P, 4, HD])
        sing = sb("p_sing", [P, 4, HD])
        ht_hi = sb("p_ht_hi", [P, 2, KD, P], F32R)
        ht_lo = sb("p_ht_lo", [P, 2, KD, P], F32R)
        qn = sb("p_qn", [P, 512])
        rot = sb("p_rot", [P, 512])
        qr = sb("p_qr", [P, 512])
        qk_st = sb("p_qk_st", [P, 2, 512])
        v_st = sb("p_v_st", [P, 512])
        vb_st = sb("p_vb_st", [P, P])
        st = sb("p_st", [P, 64])
        ps_mm = ctx.enter_context(nc.psum_tensor("p_ps_mm", [P, 2, BANK], F32))
        ps_t = ctx.enter_context(nc.psum_tensor("p_ps_t", [P, 2, BANK], F32))
        ps_x = ctx.enter_context(nc.psum_tensor("p_ps_x", [P, KD, P], F32))
        sq = ctx.enter_context(nc.psum_tensor("p_ps_sq", [P, BANK], F32))

        w_loaded = [sem("p_w_loaded0"), sem("p_w_loaded1")]
        x_loaded = [sem("p_x_loaded0"), sem("p_x_loaded1")]
        trig_loaded = [sem("p_trig_loaded0"), sem("p_trig_loaded1")]
        gains_loaded = sem("p_gains_loaded")
        w_hi_done, w_lo_done = sem("p_w_hi_done"), sem("p_w_lo_done")
        x_squared, x_rms, x_normed, x_turned = (sem(f"p_x_{n}") for n in ("squared", "rms", "normed", "turned"))
        ht_hi_done, ht_lo_done = sem("p_ht_hi_done"), sem("p_ht_lo_done")
        tables_done, projected = sem("p_tables_done"), sem("p_projected")
        q_squared, q_summed, q_rms, q_scaled = (sem(f"p_q_{n}") for n in ("squared", "summed", "rms", "scaled"))
        q_roped, q_turned, q_staged = (sem(f"p_q_{n}") for n in ("roped", "turned", "staged"))
        q_stored = [sem("p_q_stored0"), sem("p_q_stored1")]
        v_stored, vb_copied, vb_stored = sem("p_v_stored"), sem("p_vb_copied"), sem("p_vb_stored")
        norm_chain, rope_chain = sem("p_norm_chain"), sem("p_rope_chain")
        va_copied = sem("p_va_copied")

        ssq, rms, rstd = st[:, 0:2], st[:, 2:4], st[:, 4:6]
        q_ssq, q_rt, q_rs = st[:, 16:24], st[:, 24:32], st[:, 32:40]
        w_src = io["w_in"].rearrange("l (k p) n -> p l k n", p=P)

        def tiles(eng, tile):
            with eng.Fori(0, TILES // 2 - 1) as j:
                for b in range(2):
                    tile(j * 2 + b, b, j, True)
            tile(TILES - 2, 0, TILES // 2 - 1, True)
            tile(TILES - 1, 1, TILES // 2 - 1, False)

        def bank(b, c):
            return (NCH * b + c) % 2

        with nc.Block() as block:
            @block.sync
            def _(sp):
                sp.dma_start(gain_x[:], io["attn_norm"][bass.ds(layer, 1), :].squeeze(0).partition_broadcast(P)).then_inc(gains_loaded, 16)
                for g, name in enumerate(("q_norm_a", "k_norm_a", "q_norm_b", "k_norm_b")):
                    sp.dma_start(gains[:, g, :], io[name][bass.ds(layer, 1), :].squeeze(0).partition_broadcast(P)).then_inc(gains_loaded, 16)

                def load_x(i, b):
                    if warm(i):
                        sp.wait_ge(x_turned, i - 1)
                        sp.wait_ge(tables_done, i - 1)
                    sp.dma_start(x_in[:, b, :], io["y"][bass.ds(i * P, P), :]).then_inc(x_loaded[b], 16)
                    sp.dma_start(trig[:, b, :, :], io["trig"][bass.ds(i * P, P), :].rearrange("p (t d) -> p t d", t=2)).then_inc(trig_loaded[b], 16)

                load_x(0, 0)
                for n, pc in enumerate(pieces):
                    if n >= 2:
                        sp.wait_ge(w_lo_done, n - 1)
                    sp.dma_start(w_raw[:, n % 2], w_src[:, bass.ds(layer, 1), :, pc * CH:(pc + 1) * CH].squeeze(1)).then_inc(w_loaded[n % 2], 16)

                def tile(i, b, j, more):
                    if more:
                        load_x(i + 1, 1 - b)
                    for c, (_, heads, _, blk, vcol) in enumerate(CHUNKS):
                        if heads:
                            nb = heads // 2
                            sp.wait_ge(q_staged, i * 4 + c + 1)
                            sp.sem_inc(io["held"], 1)
                            sp.dma_start(io["qkT"][blk:blk + nb, :, bass.ds(i * P, P)].rearrange("c p t -> p c t"),
                                         qk_st[:, c % 2, 0:nb * P].rearrange("p (c t) -> p c t", c=nb)).then_inc(q_stored[c % 2], 16)
                        if vcol == 512:
                            sp.wait_ge(vb_copied, i + 1)
                            sp.dma_start(io["v"][bass.ds(i * P, P), 512:640], vb_st[:]).then_inc(vb_stored, 16)
                        if vcol == 0:
                            sp.wait_ge(va_copied, i + 1)
                            sp.sem_inc(io["held"], 1)
                            sp.dma_start(io["v"][bass.ds(i * P, P), 0:512], v_st[:]).then_inc(v_stored, 16)
                tiles(sp, tile)
                for s in q_stored:
                    sp.wait_ge(s, 32 * TILES)
                sp.wait_ge(vb_stored, 16 * TILES)
                sp.wait_ge(v_stored, 16 * TILES)

            @block.scalar
            def _(act):
                def prepare(i, b, j):
                    act.wait_ge(x_loaded[b], j * 16 + 16)
                    act.wait_ge(ht_lo_done, i)
                    act.activation(ps_x[:].rearrange("p k t -> p (k t)"), x_in[:, b, :], ACT.Square, accum_out=ssq[:, b:b + 1]).then_inc(x_squared, 1)
                    act.wait_ge(x_squared, i + 1)
                    act.activation(rms[:, b:b + 1], ssq[:, b:b + 1], ACT.Sqrt, bias=io["eps"][:, 0:1], scale=1.0 / D).then_inc(x_rms, 1)

                def prepared(i, b):
                    act.wait_ge(x_turned, i + 1)
                    act.activation(ht_hi[:, b], ps_x[:], ACT.Copy).then_inc(ht_hi_done, 1)

                def split(n, pc):
                    act.wait_ge(w_loaded[n % 2], 16 * (n // 2 + 1))
                    act.activation(w_hi[:, :, pc * CH:(pc + 1) * CH], w_raw[:, n % 2], ACT.Copy).then_inc(w_hi_done, 1)

                prepare(0, 0, 0)
                split(0, pieces[0])
                prepared(0, 0)
                for n, pc in enumerate(pieces):
                    if n:
                        split(n, pc)

                def stage_out(i, b, c):
                    nb = CHUNKS[c][1] // 2
                    act.wait_ge(q_turned, i * 4 + c + 1)
                    act.wait_ge(q_stored[c % 2], i * 32 + 16 * (c // 2))
                    act.activation(qk_st[:, c % 2, 0:nb * P], ps_t[:, c % 2, 0:nb * P], ACT.Copy).then_inc(q_staged, 1)

                def tile(i, b, j, more):
                    for c, (_, heads, _, _, vcol) in enumerate(CHUNKS):
                        act.wait_ge(projected, i * NCH + c + 1)
                        ps = ps_mm[:, bank(b, c), :]
                        if heads:
                            act.wait_ge(q_summed, i * 4 + c)
                            act.activation(sq[:, 0:heads * HD], ps[:, 0:heads * HD], ACT.Square).then_inc(q_squared, 1)
                            act.wait_ge(q_summed, i * 4 + c + 1)
                            act.activation(q_rt[:, 0:heads], q_ssq[:, 0:heads], ACT.Sqrt, bias=io["eps"][:, 0:1], scale=1.0 / HD).then_inc(q_rms, 1)
                        if vcol == 0:
                            act.wait_ge(v_stored, i * 16)
                            act.activation(v_st[:], ps, ACT.Copy).then_inc(va_copied, 1)
                        if c:
                            stage_out(i, b, c - 1)
                        if c == 1 and more:
                            prepare(i + 1, 1 - b, j + b)
                        if c == 3 and more:
                            prepared(i + 1, 1 - b)
                tiles(act, tile)

            @block.vector
            def _(dve):
                dve.wait_ge(gains_loaded, 16 * 5)

                def prepare(i, b, j):
                    dve.wait_ge(x_rms, i + 1)
                    ch = Chain(dve, norm_chain, i, 1)
                    ch.link(dve.reciprocal(rstd[:, b:b + 1], rms[:, b:b + 1]))
                    ch.close()
                    dve.scalar_tensor_tensor(x_in[:, b, :], x_in[:, b, :], rstd[:, b:b + 1], gain_x[:], ALU.mult, ALU.mult).then_inc(x_normed, 1)

                def prepared(i, b):
                    dve.wait_ge(ht_hi_done, i + 1)
                    dve.tensor_tensor(ht_lo[:, b], ps_x[:], ht_hi[:, b].bitcast(F32), ALU.subtract).then_inc(ht_lo_done, 1)

                def split(n, pc):
                    dve.wait_ge(w_hi_done, n + 1)
                    c0 = pc * CH
                    dve.tensor_tensor(w_lo[:, :, c0:c0 + CH], w_raw[:, n % 2], w_hi[:, :, c0:c0 + CH].bitcast(F32), ALU.subtract).then_inc(w_lo_done, 1)

                prepare(0, 0, 0)
                split(0, pieces[0])
                prepared(0, 0)
                for n, pc in enumerate(pieces):
                    if n:
                        split(n, pc)

                def tile(i, b, j, more):
                    dve.wait_ge(trig_loaded[b], j * 16 + 16)
                    dve.wait_ge(q_roped, i * 4)
                    dve.tensor_tensor(cosg[:], gains[:], over(trig[:, b, 0, :], 4), ALU.mult)
                    dve.tensor_tensor(sing[:, :, 0:HALF], gains[:, :, HALF:HD], over(trig[:, b, 1, 0:HALF], 4), ALU.mult)
                    ch = Chain(dve, tables_done, i, 1)
                    ch.link(dve.tensor_tensor(sing[:, :, HALF:HD], gains[:, :, 0:HALF], over(trig[:, b, 1, HALF:HD], 4), ALU.mult))
                    for c, (_, heads, g, _, vcol) in enumerate(CHUNKS):
                        if heads:
                            w = heads * HD
                            ps = ps_mm[:, bank(b, c), 0:w].rearrange("p (h d) -> p h d", d=HD)
                            qnv, rotv, qrv = (t[:, 0:w].rearrange("p (h d) -> p h d", d=HD) for t in (qn, rot, qr))
                            n = i * 4 + c
                            dve.wait_ge(q_squared, n + 1)
                            dve.tensor_reduce(q_ssq[:, 0:heads], sq[:, 0:w].rearrange("p (h d) -> p h d", d=HD), AX_X, ALU.add).then_inc(q_summed, 1)
                            dve.wait_ge(q_rms, n + 1)
                            ch = Chain(dve, rope_chain, n, 2)
                            ch.link(dve.reciprocal(q_rs[:, 0:heads], q_rt[:, 0:heads]))
                            dve.tensor_tensor(qnv, ps, along(q_rs[:, 0:heads], HD), ALU.mult).then_inc(q_scaled, 1)
                            if vcol == 512:
                                dve.wait_ge(vb_stored, i * 16)
                                dve.tensor_copy(vb_st[:], ps_mm[:, bank(b, c), P:2 * P]).then_inc(vb_copied, 1)
                            dve.wait_ge(q_scaled, n + 1)
                            dve.wait_ge(q_turned, n)
                            dve.tensor_tensor(qrv, qnv, over(cosg[:, g, :], heads), ALU.mult)
                            dve.tensor_tensor(rotv[:, :, 0:HALF], qnv[:, :, HALF:HD], over(sing[:, g, 0:HALF], heads), ALU.mult)
                            ch.link(dve.tensor_tensor(rotv[:, :, HALF:HD], qnv[:, :, 0:HALF], over(sing[:, g, HALF:HD], heads), ALU.mult))
                            ch.close()
                            dve.tensor_tensor(qrv, qrv, rotv, ALU.add).then_inc(q_roped, 1)
                        if c == 1 and more:
                            prepare(i + 1, 1 - b, j + b)
                        if c == 3 and more:
                            prepared(i + 1, 1 - b)
                tiles(dve, tile)

            @block.tensor
            def _(pe):
                def turn_x(i, b):
                    pe.wait_ge(x_normed, i + 1)
                    for k in range(KD):
                        mm = pe.transpose(ps_x[:, k, :], x_in[:, b, k * P:(k + 1) * P], io["ident"][:])
                    mm.then_inc(x_turned, 1)

                def turn_q(i, c):
                    nb = CHUNKS[c][1] // 2
                    pe.wait_ge(q_roped, i * 4 + c + 1)
                    pe.wait_ge(q_staged, i * 4 + max(c - 1, 0))
                    for k in range(nb):
                        mm = pe.transpose(ps_t[:, c % 2, k * P:(k + 1) * P], qr[:, k * P:(k + 1) * P], io["ident"][:])
                    mm.then_inc(q_turned, 1)

                turn_x(0, 0)

                def tile(i, b, j, more):
                    pe.wait_ge(ht_lo_done, i + 1)
                    for c, (c0, heads, _, _, vcol) in enumerate(CHUNKS):
                        w = 256 if vcol == 512 else 512
                        pe.wait_ge(w_lo_done, SPLIT_BY[c])
                        if c == 0:
                            pe.wait_ge(q_scaled, i * 4)
                            pe.wait_ge(vb_copied, i)
                        elif c == 1:
                            pe.wait_ge(va_copied, i)
                        else:
                            pe.wait_ge(q_scaled, i * 4 + c - 1)
                        ps = ps_mm[:, bank(b, c), 0:w]
                        for k in range(KD):
                            mm = split_matmul(pe, ps, (ht_hi[:, b, k, :], ht_lo[:, b, k, :]),
                                              (w_hi[:, k, c0:c0 + w], w_lo[:, k, c0:c0 + w]), k == 0, k == KD - 1)
                        mm.then_inc(projected, 1)
                        if c:
                            turn_q(i, c - 1)
                        if c == 2 and more:
                            turn_x(i + 1, 1 - b)
                tiles(pe, tile)


def stage_dense(nc, sem, layer, io, off, S):
    T, KB = S // P, S // P
    N = DA_HEADS * T
    CW = min(S, BANK)
    tag = f"d{off}_"
    with ExitStack() as ctx:
        def sb(name, shape, dt=F32):
            return ctx.enter_context(nc.sbuf_tensor(tag + name, shape, dt))

        def sem_(name):
            return sem(tag + name)

        k_raw, v_raw = sb("k_raw", [P, S]), sb("v_raw", [P, KB, P])
        k_hi, k_lo = sb("k_hi", [P, S], F32R), sb("k_lo", [P, S], F32R)
        v_hi, v_lo = sb("v_hi", [P, DA_HEADS, KB, P], F32R), sb("v_lo", [P, DA_HEADS, KB, P], F32R)
        q_raw = sb("q_raw", [P, 2, P])
        q_hi, q_lo = sb("q_hi", [P, 2, P], F32R), sb("q_lo", [P, 2, P], F32R)
        e = sb("e", [P, 2, 2, S])
        at_hi, at_lo = sb("at_hi", [P, KB, P], F32R), sb("at_lo", [P, KB, P], F32R)
        st = sb("st", [P, 32])
        lam_v = sb("lam_v", [P, 4, HD])
        lam = sb("lam", [P, 8])
        ps_s = ctx.enter_context(nc.psum_tensor(tag + "ps_s", [P, 2, 1024], F32))
        ps_t = ctx.enter_context(nc.psum_tensor(tag + "ps_t", [P, 8, P], F32))
        ps_o = ctx.enter_context(nc.psum_tensor(tag + "ps_o", [P, 2, BANK], F32))

        q_loaded = [sem_("q_loaded0"), sem_("q_loaded1")]
        kv_loaded, v_loaded, k_split, v_split = (sem_(n) for n in ("k_loaded", "v_loaded", "k_split", "v_split"))
        k_hi_done, v_hi_done, q_hi_done, q_lo_done = (sem_(n) for n in ("k_hi_done", "v_hi_done", "q_hi_done", "q_lo_done"))
        scored, max_done, exp_done = sem_("scored"), sem_("max_done"), sem_("exp_done")
        coef_done, combined, turned = sem_("coef_done"), sem_("combined"), sem_("turned")
        at_hi_done, at_lo_done, valued, stored = (sem_(n) for n in ("at_hi_done", "at_lo_done", "valued", "stored"))
        max_chain, coef_chain = sem_("max_chain"), sem_("coef_chain")
        lam_loaded, lam_dots, lam_exps, lam_chain = (sem_(n) for n in ("lam_loaded", "lam_dots", "lam_exps", "lam_chain"))

        def mx(b):
            return st[:, 2 * b:2 * b + 2]

        def neg_max(b):
            return st[:, 4 + 2 * b:6 + 2 * b]

        def sums(b):
            return st[:, 8 + 2 * b:10 + 2 * b]

        def inv(b):
            return st[:, 12 + 2 * b:14 + 2 * b]

        def coef(b):
            return st[:, 16 + b:17 + b]

        def steps(eng, step):
            if T % 2 or DA_HEADS * T <= 8:
                for n in range(N + 3):
                    step(n // T, n % T, n, lambda k, n=n: 0 <= n - k < N)
                return
            for t in range(T):
                step(0, t, t, lambda k, t=t: t - k >= 0)
            with eng.Fori(1, DA_HEADS) as h:
                for t in range(T):
                    step(h, t, h * T + t, lambda k: True)
            for t in range(3):
                step(DA_HEADS, t, N + t, lambda k, t=t: t - k < 0)

        def back(h, t, k):
            n = t - k
            return (h, n) if n >= 0 else ((h - 1, n + T) if n + T >= 0 else (h - 2, n + 2 * T))

        with nc.Block() as block:
            @block.sync
            def _(sp):
                for r, name in enumerate(("lambda_q1", "lambda_k1", "lambda_q2", "lambda_k2")):
                    sp.dma_start(lam_v[:, r, :], io[name][bass.ds(layer, 1), :].squeeze(0).partition_broadcast(P)).then_inc(lam_loaded, 16)

                def load_q(h, t, n):
                    if warm(n):
                        sp.wait_ge(q_lo_done, n - 1)
                    sp.dma_start(q_raw[:, t % 2, :], io["qkT"][bass.ds(h, 1), :, off + t * P:off + (t + 1) * P].squeeze(0)).then_inc(q_loaded[t % 2], 16)

                def step(h, t, n, on):
                    if on(0) and t == 0:
                        sp.wait_ge(k_split, h)
                        sp.dma_start(k_raw[:], io["qkT"][bass.ds(h + 4, 1), :, off:off + S].squeeze(0)).then_inc(kv_loaded, 16)
                        sp.wait_ge(v_split, h)
                        sp.dma_start(v_raw[:], io["v"][off:off + S, bass.ds(h * P, P)].rearrange("(k p) d -> p k d", p=P)).then_inc(v_loaded, 16)
                    if on(0):
                        load_q(h, t, n)
                steps(sp, step)

            @block.scalar
            def _(act):
                act.wait_ge(lam_dots, 1)
                act.activation(lam[:, 2:4], lam[:, 0:2], ACT.Exp).then_inc(lam_exps, 1)

                def step(h, t, n, on):
                    b = t % 2
                    if on(0) and t == 0:
                        act.wait_ge(kv_loaded, h * 16 + 16)
                        act.wait_ge(scored, h * T * 2)
                        act.activation(k_hi[:], k_raw[:], ACT.Copy).then_inc(k_hi_done, 1)
                    if on(0):
                        act.wait_ge(q_loaded[b], h * (8 * T) + (t // 2) * 16 + 16)
                        if warm(n):
                            act.wait_ge(scored, n * 2 - 2)
                        act.activation(q_hi[:, b, :], q_raw[:, b, :], ACT.Copy).then_inc(q_hi_done, 1)
                    if on(0) and t == 0:
                        act.wait_ge(v_loaded, h * 16 + 16)
                        act.activation(v_hi[:, bass.ds(h, 1)].squeeze(1) if not isinstance(h, int) else v_hi[:, h], v_raw[:], ACT.Copy).then_inc(v_hi_done, 1)
                    if on(2):
                        act.wait_ge(turned, n - 1)
                        if on(3):
                            act.wait_ge(valued, n - 2)
                        act.activation(at_hi[:], ps_t[:, 0:KB, :], ACT.Copy).then_inc(at_hi_done, 1)
                    if on(0):
                        for c in range(2):
                            act.wait_ge(max_done, n * 2 + c + 1)
                            if warm(n):
                                act.wait_ge(turned, n - 1)
                                act.wait_ge(combined, n - 1)
                            act.activation(e[:, b, c, :], ps_s[:, c, 0:S], ACT.Exp, bias=neg_max(b)[:, c:c + 1],
                                           scale=SCALE, accum_out=sums(b)[:, c:c + 1]).then_inc(exp_done, 1)
                steps(act, step)

            @block.vector
            def _(dve):
                dve.wait_ge(lam_loaded, 64)
                ch = Chain(dve, lam_chain, 0, 4)
                pairs = lam_v[:].rearrange("p (a b) d -> p a b d", b=2)
                ch.link(dve.tensor_tensor(pairs[:, :, 0, :], pairs[:, :, 0, :], pairs[:, :, 1, :], ALU.mult))
                dve.tensor_reduce(lam[:, 0:2], pairs[:, :, 0, :], AX_X, ALU.add).then_inc(lam_dots, 1)
                dve.wait_ge(lam_exps, 1)
                ch.link(dve.tensor_tensor(lam[:, 4:5], lam[:, 3:4], lam[:, 2:3], ALU.subtract))
                ch.link(dve.tensor_scalar(lam[:, 6:7], io["lam_init"][:, bass.ds(layer, 1)], -1.0, None, ALU.mult))
                ch.link(dve.tensor_tensor(lam[:, 5:6], lam[:, 4:5], lam[:, 6:7], ALU.add))
                ch.close()

                def step(h, t, n, on):
                    b = t % 2
                    if on(0) and t == 0:
                        dve.wait_ge(k_hi_done, h + 1)
                        dve.tensor_tensor(k_lo[:], k_raw[:], k_hi[:].bitcast(F32), ALU.subtract).then_inc(k_split, 1)
                    if on(0):
                        dve.wait_ge(q_hi_done, n + 1)
                        dve.tensor_tensor(q_lo[:, b, :], q_raw[:, b, :], q_hi[:, b, :].bitcast(F32), ALU.subtract).then_inc(q_lo_done, 1)
                    if on(0) and t == 0:
                        dve.wait_ge(v_hi_done, h + 1)
                        vh, vl = (v[:, h] if isinstance(h, int) else v[:, bass.ds(h, 1)].squeeze(1) for v in (v_hi, v_lo))
                        dve.tensor_tensor(vl, v_raw[:], vh.bitcast(F32), ALU.subtract).then_inc(v_split, 1)
                    if on(2):
                        dve.wait_ge(at_hi_done, n - 1)
                        dve.tensor_tensor(at_lo[:], ps_t[:, 0:KB, :], at_hi[:].bitcast(F32), ALU.subtract).then_inc(at_lo_done, 1)
                    if on(3):
                        hb, tb = back(h, t, 3)
                        dve.wait_ge(valued, n - 2)
                        dve.tensor_scalar(io["mix"][:, off // P + tb, bass.ds(hb * P, P)], ps_o[:, (tb % 2), 0:P], inv(tb % 2)[:, 0:1], None, ALU.mult).then_inc(stored, 1)
                    if on(1):
                        b1 = 1 - b
                        dve.wait_ge(exp_done, n * 2)
                        if on(3):
                            dve.wait_ge(stored, n - 2)
                        ch = Chain(dve, coef_chain, n - 1, 1)
                        ch.link(dve.reciprocal(inv(b1), sums(b1)))
                        ch.close()
                        dve.scalar_tensor_tensor(coef(b1), sums(b1)[:, 0:1], lam[:, 5:6], inv(b1)[:, 1:2], ALU.mult, ALU.mult).then_inc(coef_done, 1)
                        dve.wait_ge(coef_done, n)
                        dve.scalar_tensor_tensor(e[:, b1, 0, :], e[:, b1, 1, :], coef(b1), e[:, b1, 0, :], ALU.mult, ALU.add).then_inc(combined, 1)
                    if on(0):
                        ch = Chain(dve, max_chain, n, 2)
                        for c in range(2):
                            dve.wait_ge(scored, n * 2 + c + 1)
                            ch.link(dve.tensor_reduce(mx(b)[:, c:c + 1], ps_s[:, c, 0:S], AX_X, ALU.max))
                            dve.tensor_scalar(neg_max(b)[:, c:c + 1], mx(b)[:, c:c + 1], -SCALE, None, ALU.mult).then_inc(max_done, 1)
                        ch.close()
                steps(dve, step)

            @block.tensor
            def _(pe):
                def step(h, t, n, on):
                    b = t % 2
                    if on(0):
                        pe.wait_ge(k_split, h + 1)
                        pe.wait_ge(q_lo_done, n + 1)
                        if on(1):
                            pe.wait_ge(exp_done, n * 2)
                        for (qa, ka), last in (((q_hi, k_hi), False), ((q_hi, k_lo), False), ((q_lo, k_hi), True)):
                            for c0 in range(0, S, CW):
                                for c in range(2):
                                    rows = slice(c * HD, (c + 1) * HD)
                                    mm = pe.matmul(ps_s[:, c, c0:c0 + CW], qa[rows, b, :], ka[rows, c0:c0 + CW],
                                                   start=qa is q_hi and ka is k_hi, stop=last)
                                    if last and c0 + CW == S:
                                        mm.then_inc(scored, 1)
                    if on(2):
                        hb, tb = back(h, t, 2)
                        pe.wait_ge(v_split, hb + 1)
                        pe.wait_ge(at_lo_done, n - 1)
                        if on(4):
                            pe.wait_ge(stored, n - 3)
                        for k in range(KB):
                            mm = split_matmul(pe, ps_o[:, tb % 2, 0:P], (at_hi[:, k, :], at_lo[:, k, :]),
                                              tuple(v[:, hb, k, :] if isinstance(hb, int) else v[:, bass.ds(hb, 1), k, :].squeeze(1) for v in (v_hi, v_lo)),
                                              k == 0, k == KB - 1)
                        mm.then_inc(valued, 1)
                    if on(1):
                        b1 = 1 - b
                        pe.wait_ge(combined, n)
                        if on(2):
                            pe.wait_ge(at_lo_done, n - 1)
                        for k in range(KB):
                            mm = pe.transpose(ps_t[:, k, :], e[:, b1, 0, k * P:(k + 1) * P], io["ident"][:])
                        mm.then_inc(turned, 1)
                steps(pe, step)


def stage_window(nc, sem, layer, io):
    NB = TILES + 3
    W3 = 3 * P
    N = TILES * SW_KV
    with ExitStack() as ctx:
        def sb(name, shape, dt=F32):
            return ctx.enter_context(nc.sbuf_tensor("w_" + name, shape, dt))

        def sem_(name):
            return sem("w_" + name)

        k_raw = sb("k_raw", [HD, SW_KV, NB, P])
        k_hi, k_lo = sb("k_hi", [HD, SW_KV, NB, P], F32R), sb("k_lo", [HD, SW_KV, NB, P], F32R)
        v_raw = sb("v_raw", [P, NB, P])
        v_hi, v_lo = sb("v_hi", [P, NB, P], F32R), sb("v_lo", [P, NB, P], F32R)
        q_raw = sb("q_raw", [HD, 2, GROUP, P])
        q_hi, q_lo = sb("q_hi", [HD, 2, GROUP, P], F32R), sb("q_lo", [HD, 2, GROUP, P], F32R)
        masks = sb("masks", [P, 2, TILES, P], BF16)
        identb = sb("identb", [P, P], BF16)
        e = sb("e", [P, 2, GROUP, W3])
        at_hi, at_lo = sb("at_hi", [P, 3, GROUP, P], F32R), sb("at_lo", [P, 3, GROUP, P], F32R)
        sink, neg_sink = sb("sink", [P, 8]), sb("neg_sink", [P, 8])
        st = sb("st", [P, 2, 32])
        ps_s = ctx.enter_context(nc.psum_tensor("w_ps_s", [P, GROUP, BANK], F32))
        ps_t = ctx.enter_context(nc.psum_tensor("w_ps_t", [P, 3, GROUP, P], F32))
        ps_o = ctx.enter_context(nc.psum_tensor("w_ps_o", [P, GROUP, HD], F32))

        const_loaded, keys_loaded, keys_zeroed = sem_("const_loaded"), sem_("keys_loaded"), sem_("keys_zeroed")
        k_hi_done, k_split, v_hi_done, v_split = (sem_(n) for n in ("k_hi_done", "k_split", "v_hi_done", "v_split"))
        sink_done = sem_("sink_done")
        q_loaded = [sem_("q_loaded0"), sem_("q_loaded1")]
        q_hi_done, q_lo_done, scored, max_done = (sem_(n) for n in ("q_hi_done", "q_lo_done", "scored", "max_done"))
        exp_done, inv_done, turned, at_hi_done = (sem_(n) for n in ("exp_done", "inv_done", "turned", "at_hi_done"))
        at_lo_done, valued, stored = sem_("at_lo_done"), sem_("valued"), sem_("stored")
        max_chain, inv_chain = sem_("max_chain"), sem_("inv_chain")

        def first_block(t):
            return t if not isinstance(t, int) or t < 8 else t + 1

        def steps(eng, step):
            for t in range(2):
                for n in range(2):
                    step(t, n, 2 * t + n, lambda k, u=2 * t + n: u - k >= 0)
            with eng.Fori(2, 8) as t:
                for n in range(2):
                    step(t, n, t * 2 + n, lambda k: True)
            for u in range(16, N + 3):
                step(u // 2, u % 2, u, lambda k, u=u: u - k < N)

        with nc.Block() as block:
            @block.gpsimd
            def _(pool):
                for blk in (0, 9, NB - 1):
                    nc.gpsimd.memset(k_raw[:, :, blk, :], 0.0)
                    last = nc.gpsimd.memset(v_raw[:, blk, :], 0.0)
                last.then_inc(keys_zeroed, 1)

            @block.sync
            def _(sp):
                sp.dma_start(masks[:], io["masks"].rearrange("s t q k -> q s t k")).then_inc(const_loaded, 16)
                sp.dma_start(identb[:], io["identb"]).then_inc(const_loaded, 16)
                sp.dma_start(sink[:], io["sink_b"][bass.ds(layer, 1), :].squeeze(0).partition_broadcast(P)).then_inc(const_loaded, 16)
                for lo, n, r0 in ((1, 8, 0), (10, 2, PROMPT)):
                    sp.dma_start(k_raw[:, :, lo:lo + n, :].rearrange("d h b t -> d h (b t)"),
                                 io["qkT"][12, :, r0:r0 + n * P].rearrange("(h d) t -> d h t", d=HD)).then_inc(keys_loaded, 16)
                    sp.dma_start(v_raw[:, lo:lo + n, :], io["v"][r0:r0 + n * P, 512:640].rearrange("(b p) d -> p b d", p=P)).then_inc(keys_loaded, 16)

                def step(t, n, u, on):
                    if on(0):
                        if warm(u):
                            sp.wait_ge(q_lo_done, u - 1)
                        r0 = t * P
                        sp.dma_start(q_raw[:, n], io["qkT"][8 + 2 * n:10 + 2 * n, :, bass.ds(r0, P)].rearrange("c (g d) t -> d (c g) t", d=HD)).then_inc(q_loaded[n], 16)
                steps(sp, step)

            @block.scalar
            def _(act):
                act.wait_ge(keys_zeroed, 1)
                act.wait_ge(keys_loaded, 64)
                act.activation(k_hi[:], k_raw[:], ACT.Copy).then_inc(k_hi_done, 1)
                act.activation(v_hi[:], v_raw[:], ACT.Copy).then_inc(v_hi_done, 1)

                def step(t, n, u, on):
                    if on(0):
                        act.wait_ge(q_loaded[n], t * 16 + 16)
                        if warm(u):
                            act.wait_ge(scored, u - 1)
                        act.activation(q_hi[:, n], q_raw[:, n], ACT.Copy).then_inc(q_hi_done, 1)
                    if on(2):
                        act.wait_ge(turned, u - 1)
                        if on(3):
                            act.wait_ge(valued, u - 2)
                        act.activation(at_hi[:], ps_t[:], ACT.Copy).then_inc(at_hi_done, 1)
                    if on(0):
                        act.wait_ge(max_done, u + 1)
                        if warm(u):
                            act.wait_ge(turned, u - 1)
                            act.wait_ge(inv_done, u - 1)
                        for g in range(GROUP):
                            act.activation(e[:, n, g, :], ps_s[:, g, 0:W3], ACT.Exp, bias=st[:, n, 4 + g:5 + g], scale=SCALE, accum_out=st[:, n, 8 + g:9 + g])
                        act.activation(st[:, n, 16:20], st[:, n, 12:16], ACT.Exp).then_inc(exp_done, 1)
                steps(act, step)

            @block.vector
            def _(dve):
                dve.wait_ge(const_loaded, 48)
                dve.tensor_scalar(neg_sink[:], sink[:], -1.0, None, ALU.mult).then_inc(sink_done, 1)
                dve.wait_ge(k_hi_done, 1)
                dve.tensor_tensor(k_lo[:], k_raw[:], k_hi[:].bitcast(F32), ALU.subtract).then_inc(k_split, 1)
                dve.wait_ge(v_hi_done, 1)
                dve.tensor_tensor(v_lo[:], v_raw[:], v_hi[:].bitcast(F32), ALU.subtract).then_inc(v_split, 1)
                dve.wait_ge(sink_done, 1)

                def step(t, n, u, on):
                    if on(0):
                        dve.wait_ge(q_hi_done, u + 1)
                        dve.tensor_tensor(q_lo[:, n], q_raw[:, n], q_hi[:, n].bitcast(F32), ALU.subtract).then_inc(q_lo_done, 1)
                    if on(2):
                        dve.wait_ge(at_hi_done, u - 1)
                        dve.tensor_tensor(at_lo[:], ps_t[:], at_hi[:].bitcast(F32), ALU.subtract).then_inc(at_lo_done, 1)
                    if on(3):
                        n3 = 1 - n
                        t3 = t - 1 if n == 1 else t - 2
                        dve.wait_ge(valued, u - 2)
                        dve.tensor_tensor(io["mix"][:, bass.ds(t3, 1), 512 + n3 * 256:768 + n3 * 256].rearrange("p a (g d) -> p (a g) d", g=GROUP), ps_o[:],
                                          along(st[:, n3, 24:28], HD), ALU.mult).then_inc(stored, 1)
                    if on(1):
                        n1 = 1 - n
                        dve.wait_ge(exp_done, u)
                        ch = Chain(dve, inv_chain, u - 1, 1)
                        ch.link(dve.tensor_tensor(st[:, n1, 20:24], st[:, n1, 8:12], st[:, n1, 16:20], ALU.add))
                        ch.close()
                        dve.reciprocal(st[:, n1, 24:28], st[:, n1, 20:24]).then_inc(inv_done, 1)
                    if on(0):
                        dve.wait_ge(scored, u + 1)
                        ch = Chain(dve, max_chain, u, 2)
                        ch.link(dve.tensor_reduce(st[:, n, 0:4], ps_s[:, :, 0:W3], AX_X, ALU.max))
                        ch.link(dve.scalar_tensor_tensor(st[:, n, 4:8], st[:, n, 0:4], -SCALE, neg_sink[:, n * 4:n * 4 + 4], ALU.mult, ALU.min))
                        ch.close()
                        dve.tensor_tensor(st[:, n, 12:16], st[:, n, 4:8], sink[:, n * 4:n * 4 + 4], ALU.add).then_inc(max_done, 1)
                steps(dve, step)

            @block.tensor
            def _(pe):
                pe.wait_ge(const_loaded, 48)
                pe.wait_ge(k_split, 1)
                pe.wait_ge(v_split, 1)

                def step(t, n, u, on):
                    if on(0):
                        pe.wait_ge(q_lo_done, u + 1)
                        if on(1):
                            pe.wait_ge(exp_done, u)
                        kb = first_block(t)
                        kh, kl = (k[:, n, bass.ds(kb, 3), :].rearrange("d b t -> d (b t)") for k in (k_hi, k_lo))
                        for g in range(GROUP):
                            out = ps_s[:, g, 0:W3]
                            pe.matmul(out, q_hi[:, n, g, :], kh, start=True, stop=False)
                            pe.matmul(out, q_hi[:, n, g, :], kl, start=False, stop=False)
                            for side, c0 in ((0, 0), (1, 2 * P)):
                                pe.matmul(ps_s[:, g, c0:c0 + P], identb[:], masks[:, side, t, :] if isinstance(t, int) else masks[:, side, bass.ds(t, 1), :].squeeze(1),
                                          start=False, stop=False, skip_group_check=True)
                            mm = pe.matmul(out, q_lo[:, n, g, :], kh, start=False, stop=True)
                        mm.then_inc(scored, 1)
                    if on(2):
                        t2 = t - 1
                        pe.wait_ge(at_lo_done, u - 1)
                        if on(3):
                            pe.wait_ge(stored, u - 2)
                        fb = first_block(t2)
                        for g in range(GROUP):
                            for k in range(3):
                                vh, vl = (v[:, bass.ds(fb + k, 1), n * HD:(n + 1) * HD].squeeze(1) for v in (v_hi, v_lo))
                                mm = split_matmul(pe, ps_o[:, g, :], (at_hi[:, k, g, :], at_lo[:, k, g, :]), (vh, vl), k == 0, k == 2)
                        mm.then_inc(valued, 1)
                    if on(1):
                        pe.wait_ge(exp_done, u)
                        if on(2):
                            pe.wait_ge(at_lo_done, u - 1)
                        for k in range(3):
                            for g in range(GROUP):
                                mm = pe.transpose(ps_t[:, k, g, :], e[:, 1 - n, g, k * P:(k + 1) * P], io["ident"][:])
                        mm.then_inc(turned, 1)
                steps(pe, step)


def stage_mix(nc, sem, layer, io):
    RK = 2
    with ExitStack() as ctx:
        def sb(name, shape, dt=F32):
            return ctx.enter_context(nc.sbuf_tensor("m_" + name, shape, dt))

        def sem_(name):
            return sem("m_" + name)

        w_raw = sb("w_raw", [P, 2, RK, D])
        w_hi, w_lo = sb("w_hi", [P, KD, D], F32R), sb("w_lo", [P, KD, D], F32R)
        r_raw = sb("r_raw", [P, KD, E])
        r_hi, r_lo = sb("r_hi", [P, KD, E], F32R), sb("r_lo", [P, KD, E], F32R)
        gain_h = sb("gain_h", [P, D])
        subln = sb("subln", [P, P])
        subg = sb("subg", [P, P])
        mixn = sb("mixn", [P, D])
        sq = sb("sq", [P, 512])
        mt_hi, mt_lo = sb("mt_hi", [P, KD, P], F32R), sb("mt_lo", [P, KD, P], F32R)
        ht_hi, ht_lo = sb("ht_hi", [P, KD, P], F32R), sb("ht_lo", [P, KD, P], F32R)
        x = sb("x", [P, 2, D])
        h = sb("h", [P, 2, D])
        st = sb("st", [P, 48])
        ps_m = ctx.enter_context(nc.psum_tensor("m_ps_m", [P, KD, P], F32))
        ps_h = ctx.enter_context(nc.psum_tensor("m_ps_h", [P, KD, P], F32))
        ps_o = ctx.enter_context(nc.psum_tensor("m_ps_o", [P, D], F32))
        ps_r = ctx.enter_context(nc.psum_tensor("m_ps_r", [P, BANK], F32))

        consts_loaded, w_hi_done, w_lo_done, r_hi_done, r_lo_done = (sem_(n) for n in ("consts_loaded", "w_hi_done", "w_lo_done", "r_hi_done", "r_lo_done"))
        subg_done = sem_("subg_done")
        w_loaded = [sem_("w_loaded0"), sem_("w_loaded1")]
        x_loaded = [sem_("x_loaded0"), sem_("x_loaded1")]
        x_stored = [sem_("x_stored0"), sem_("x_stored1")]
        h_stored = [sem_("h_stored0"), sem_("h_stored1")]
        squared, summed, rooted, mix_ready = (sem_(n) for n in ("squared", "summed", "rooted", "mix_ready"))
        mix_turned, mt_hi_done, mt_lo_done, mixed = (sem_(n) for n in ("mix_turned", "mt_hi_done", "mt_lo_done", "mixed"))
        x_done, x_squared, x_rooted, h_done = (sem_(n) for n in ("x_done", "x_squared", "x_rooted", "h_done"))
        h_turned, ht_hi_done, ht_lo_done, routed, logits_done = (sem_(n) for n in ("h_turned", "ht_hi_done", "ht_lo_done", "routed", "logits_done"))
        sub_chain, h_chain = sem_("sub_chain"), sem_("h_chain")

        with nc.Block() as block:
            @block.sync
            def _(sp):
                sp.dma_start(subln[:], io["subln_a"][bass.ds(layer, 1), :].squeeze(0).partition_broadcast(P)).then_inc(consts_loaded, 16)
                sp.dma_start(gain_h[:], io["ffn_norm"][bass.ds(layer, 1), :].squeeze(0).partition_broadcast(P)).then_inc(consts_loaded, 16)
                sp.dma_start(r_raw[:], io["w_router"][bass.ds(layer, 1)].squeeze(0).rearrange("(k p) e -> p k e", p=P)).then_inc(consts_loaded, 16)
                for n in range(KD // RK):
                    if n >= 2:
                        sp.wait_ge(w_lo_done, n - 1)
                    sp.dma_start(w_raw[:, n % 2], io["w_out"][bass.ds(layer, 1), n * RK * P:(n + 1) * RK * P, :].squeeze(0).rearrange("(k p) n -> p k n", p=P)).then_inc(w_loaded[n % 2], 16)

                def step(i, b, on, j=None):
                    if on(0):
                        if warm(i):
                            sp.wait_ge(x_stored[b], 16 * j)
                            sp.wait_ge(h_done, i - 1)
                        sp.dma_start(x[:, b, :], io["y"][bass.ds(i * P, P), :]).then_inc(x_loaded[b], 16)
                    if on(1):
                        sp.wait_ge(x_done, i)
                        sp.dma_start(io["y"][bass.ds((i - 1) * P, P), :], x[:, 1 - b, :]).then_inc(x_stored[1 - b], 16)
                    if on(2):
                        sp.wait_ge(h_done, i - 1)
                        sp.dma_start(io["h"][bass.ds((i - 2) * P, P), :], h[:, b, :]).then_inc(h_stored[b], 16)
                paired(sp, TILES, 2, step)
                for s in x_stored + h_stored:
                    sp.wait_ge(s, 16 * TILES // 2)

            @block.scalar
            def _(act):
                act.wait_ge(consts_loaded, 48)
                act.activation(r_hi[:], r_raw[:], ACT.Copy).then_inc(r_hi_done, 1)
                for n in range(KD // RK):
                    act.wait_ge(w_loaded[n % 2], 16 * (n // 2 + 1))
                    act.activation(w_hi[:, n * RK:(n + 1) * RK, :], w_raw[:, n % 2], ACT.Copy).then_inc(w_hi_done, 1)

                def step(i, b, on, j=None):
                    if on(2):
                        act.wait_ge(h_turned, i - 1)
                        if on(3):
                            act.wait_ge(routed, i - 2)
                        act.activation(ht_hi[:], ps_h[:], ACT.Copy).then_inc(ht_hi_done, 1)
                    if on(0):
                        act.wait_ge(summed, i)
                        act.activation(sq[:], io["mix"][:, bass.ds(i, 1), 0:512].squeeze(1), ACT.Square).then_inc(squared, 1)
                        act.wait_ge(summed, i + 1)
                        act.activation(st[:, 4:8], st[:, 0:4], ACT.Sqrt, bias=io["eps"][:, 0:1], scale=1.0 / P).then_inc(rooted, 1)
                        act.wait_ge(mix_turned, i + 1)
                        if on(1):
                            act.wait_ge(mixed, i)
                        act.activation(mt_hi[:], ps_m[:], ACT.Copy).then_inc(mt_hi_done, 1)
                    if on(1):
                        act.wait_ge(x_done, i)
                        if on(3):
                            act.wait_ge(h_stored[1 - b], 16 * (j - (1 if b == 0 else 0)) if not isinstance(i, int) else 16 * ((i - 1) // 2))
                            act.wait_ge(h_turned, i - 2)
                        act.activation(h[:, 1 - b, :], x[:, 1 - b, :], ACT.Square, accum_out=st[:, 16 + 1 - b:17 + 1 - b]).then_inc(x_squared, 1)
                        act.wait_ge(x_squared, i)
                        act.activation(st[:, 18 + 1 - b:19 + 1 - b], st[:, 16 + 1 - b:17 + 1 - b], ACT.Sqrt, bias=io["eps"][:, 0:1], scale=1.0 / D).then_inc(x_rooted, 1)
                paired(act, TILES, 2, step)

            @block.vector
            def _(dve):
                dve.wait_ge(consts_loaded, 48)
                dve.tensor_scalar(subg[:], subln[:], io["lam_rest"][:, bass.ds(layer, 1)], None, ALU.mult).then_inc(subg_done, 1)
                dve.wait_ge(r_hi_done, 1)
                dve.tensor_tensor(r_lo[:], r_raw[:], r_hi[:].bitcast(F32), ALU.subtract).then_inc(r_lo_done, 1)
                for n in range(KD // RK):
                    dve.wait_ge(w_hi_done, n + 1)
                    dve.tensor_tensor(w_lo[:, n * RK:(n + 1) * RK, :], w_raw[:, n % 2], w_hi[:, n * RK:(n + 1) * RK, :].bitcast(F32), ALU.subtract).then_inc(w_lo_done, 1)
                dve.wait_ge(subg_done, 1)

                def step(i, b, on, j=None):
                    if on(2):
                        dve.wait_ge(ht_hi_done, i - 1)
                        dve.tensor_tensor(ht_lo[:], ps_h[:], ht_hi[:].bitcast(F32), ALU.subtract).then_inc(ht_lo_done, 1)
                    if on(0):
                        mix = io["mix"][:, bass.ds(i, 1), :].squeeze(1)
                        mh = mixn[:, 0:512].rearrange("p (h d) -> p h d", d=P)
                        ch = Chain(dve, sub_chain, i, 2)
                        dve.wait_ge(squared, i + 1)
                        dve.tensor_reduce(st[:, 0:4], sq[:].rearrange("p (h d) -> p h d", d=P), AX_X, ALU.add).then_inc(summed, 1)
                        dve.wait_ge(rooted, i + 1)
                        ch.link(dve.reciprocal(st[:, 8:12], st[:, 4:8]))
                        dve.wait_ge(mix_turned, i)
                        dve.tensor_copy(mixn[:, 512:1024], mix[:, 512:1024])
                        ch.link(dve.tensor_tensor(mh, mix[:, 0:512].rearrange("p (h d) -> p h d", d=P), along(st[:, 8:12], P), ALU.mult))
                        ch.close()
                        dve.tensor_tensor(mh, mh, over(subg[:], 4), ALU.mult).then_inc(mix_ready, 1)
                        dve.wait_ge(mt_hi_done, i + 1)
                        dve.tensor_tensor(mt_lo[:], ps_m[:], mt_hi[:].bitcast(F32), ALU.subtract).then_inc(mt_lo_done, 1)
                    if on(1):
                        b1 = 1 - b
                        dve.wait_ge(x_loaded[b1], 16 * ((i - 1) // 2 + 1) if isinstance(i, int) else (j * 16 if b == 0 else j * 16 + 16))
                        dve.wait_ge(mixed, i)
                        dve.tensor_tensor(x[:, b1, :], ps_o[:], x[:, b1, :], ALU.add).then_inc(x_done, 1)
                        dve.wait_ge(x_rooted, i)
                        ch = Chain(dve, h_chain, i - 1, 1)
                        ch.link(dve.reciprocal(st[:, 20 + b1:21 + b1], st[:, 18 + b1:19 + b1]))
                        ch.close()
                        dve.scalar_tensor_tensor(h[:, b1, :], x[:, b1, :], st[:, 20 + b1:21 + b1], gain_h[:], ALU.mult, ALU.mult).then_inc(h_done, 1)
                    if on(3):
                        dve.wait_ge(routed, i - 2)
                        dve.tensor_copy(io["logits"][:, bass.ds(i - 3, 1), :].squeeze(1), ps_r[:, 0:E]).then_inc(logits_done, 1)
                paired(dve, TILES, 3, step)

            @block.tensor
            def _(pe):
                pe.wait_ge(r_lo_done, 1)

                def step(i, b, on, j=None):
                    if on(2):
                        pe.wait_ge(h_done, i - 1)
                        if on(3):
                            pe.wait_ge(ht_lo_done, i - 2)
                        for k in range(KD):
                            mm = pe.transpose(ps_h[:, k, :], h[:, b, k * P:(k + 1) * P], io["ident"][:])
                        mm.then_inc(h_turned, 1)
                    if on(0):
                        pe.wait_ge(mix_ready, i + 1)
                        if on(1):
                            pe.wait_ge(mt_lo_done, i)
                        for k in range(KD):
                            mm = pe.transpose(ps_m[:, k, :], mixn[:, k * P:(k + 1) * P], io["ident"][:])
                        mm.then_inc(mix_turned, 1)
                    if on(2):
                        pe.wait_ge(ht_lo_done, i - 1)
                        if on(3):
                            pe.wait_ge(logits_done, i - 2)
                        for k in range(KD):
                            mm = split_matmul(pe, ps_r[:, 0:E], (ht_hi[:, k, :], ht_lo[:, k, :]), (r_hi[:, k, :], r_lo[:, k, :]), k == 0, k == KD - 1)
                        mm.then_inc(routed, 1)
                    if on(0):
                        pe.wait_ge(w_lo_done, KD // RK)
                        pe.wait_ge(mt_lo_done, i + 1)
                        if on(1):
                            pe.wait_ge(x_done, i)
                        for half in range(2):
                            c = slice(half * BANK, (half + 1) * BANK)
                            for k in range(KD):
                                mm = split_matmul(pe, ps_o[:, c], (mt_hi[:, k, :], mt_lo[:, k, :]), (w_hi[:, k, c], w_lo[:, k, c]), k == 0, k == KD - 1)
                        mm.then_inc(mixed, 1)
                paired(pe, TILES, 2, step)


def stage_choose(nc, sem, io):
    G = 32 + E
    R = TILES * E
    with ExitStack() as ctx:
        def sb(name, shape, dt=F32):
            return ctx.enter_context(nc.sbuf_tensor("c_" + name, shape, dt))

        def sem_(name):
            return sem("c_" + name)

        z = sb("z", [P, TILES, E])
        mx, total, inv = sb("mx", [P, TILES]), sb("total", [P, TILES]), sb("inv", [P, TILES])
        aff = sb("aff", [G, PROMPT])
        vals = sb("vals", [G, CAP_P])
        rows = sb("rows", [G, CAP_P], U32)
        rows_f = sb("rows_f", [G, CAP_P])
        ps_a = ctx.enter_context(nc.psum_tensor("c_ps_a", [E, 3, BANK], F32))
        ps_v = ctx.enter_context(nc.psum_tensor("c_ps_v", [P, BANK], F32))
        ps_i = ctx.enter_context(nc.psum_tensor("c_ps_i", [P, BANK], F32))
        soft_chain, shifted, exp_done, soft_done, cleared = (sem_(n) for n in ("soft_chain", "shifted", "exp_done", "soft_done", "cleared"))
        turned, aff_ready, top_chain, lists_ready, lists_turned = (sem_(n) for n in ("turned", "aff_ready", "top_chain", "lists_ready", "lists_turned"))
        tables_done = sem_("tables_done")

        with nc.Block() as block:
            @block.scalar
            def _(act):
                act.wait_ge(shifted, 1)
                act.activation(z[:], z[:], ACT.Exp).then_inc(exp_done, 1)
                act.wait_ge(cleared, 1)
                act.wait_ge(turned, 1)
                act.activation(aff[0:E, :].rearrange("e (a t) -> e a t", a=2), ps_a[:, 0:2, :], ACT.Copy).then_inc(aff_ready, 1)
                act.activation(aff[32:32 + E, 0:SAMPLE], ps_a[:, 2, 0:SAMPLE], ACT.Copy).then_inc(aff_ready, 1)

            @block.gpsimd
            def _(pool):
                nc.gpsimd.memset(aff[:], -1.0).then_inc(cleared, 1)

            @block.tensor
            def _(pe):
                pe.wait_ge(soft_done, 1)
                for t in range(TILES):
                    mm = pe.transpose(ps_a[:, t // 4, (t % 4) * P:(t % 4 + 1) * P], z[:, t, :], io["ident"][:])
                mm.then_inc(turned, 1)
                pe.wait_ge(lists_ready, 1)
                pe.transpose(ps_v[:, 0:G], vals[:], io["ident"][0:G, 0:G])
                pe.transpose(ps_i[:, 0:G], rows_f[:], io["ident"][0:G, 0:G]).then_inc(lists_turned, 1)

            @block.vector
            def _(dve):
                ch = Chain(dve, soft_chain, 0, 3)
                ch.link(dve.tensor_reduce(mx[:], io["logits"][:], AX_X, ALU.max))
                dve.tensor_tensor(z[:], io["logits"][:], along(mx[:], E), ALU.subtract).then_inc(shifted, 1)
                dve.wait_ge(exp_done, 1)
                ch.link(dve.tensor_reduce(total[:], z[:], AX_X, ALU.add))
                ch.link(dve.reciprocal(inv[:], total[:]))
                ch.close()
                dve.tensor_tensor(z[:], z[:], along(inv[:], E), ALU.mult).then_inc(soft_done, 1)
                dve.wait_ge(aff_ready, 2)
                rounds = CAP_P // 8
                ch = Chain(dve, top_chain, 0, 2 * rounds + 1)
                for r in range(rounds):
                    c = slice(8 * r, 8 * r + 8)
                    ch.link(dve.max(vals[:, c], aff[:]))
                    dve.max_index(rows[:, c], vals[:, c], aff[:])
                    ch.link(dve.match_replace(aff[:], vals[:, c], aff[:], -2.0))
                ch.link(dve.tensor_copy(rows_f[:], rows[:]))
                ch.close()
                nc.vector.engine_nop().then_inc(lists_ready, 1)
                dve.wait_ge(lists_turned, 1)
                dve.tensor_copy(io["vals"][:, 0, :], ps_v[:, 0:E])
                dve.tensor_copy(io["vals"][:, 1, :], ps_v[:, 32:G])
                dve.tensor_copy(io["rows"][:, 0, :], ps_i[:, 0:E])
                dve.tensor_scalar(io["rows"][:, 1, :], ps_i[:, 32:G], float(PROMPT), None, ALU.add).then_inc(tables_done, 1)


def stage_experts(nc, sem, layer, io):
    NS, CH = 12, 256
    RING = 12
    B2 = CH // P
    with ExitStack() as ctx:
        def sb(name, shape, dt=F32):
            return ctx.enter_context(nc.sbuf_tensor("e_" + name, shape, dt))

        def sem_(name):
            return sem("e_" + name)

        w = sb("w", [P, RING, KD, CH])
        xp, xs = sb("xp", [P, D]), sb("xs", [CAP_S, D])
        xt = sb("xt", [P, KD, SLOTS])
        gate = sb("gate", [P, B2, SLOTS])
        hid = sb("hid", [P, KD, SLOTS])
        yt = sb("yt", [P, 2, B2, SLOTS])
        yp, ys = sb("yp", [P, D]), sb("ys", [CAP_S, D])
        ip_g, is_g, ip_s, is_s = (sb(n, [P, 1], U32) for n in ("ip_g", "is_g", "ip_s", "is_s"))
        ps_w = ctx.enter_context(nc.psum_tensor("e_ps_w", [P, 4, BANK], F32))
        ps_x = ctx.enter_context(nc.psum_tensor("e_ps_x", [P, 2, BANK], F32))
        ps_y = ctx.enter_context(nc.psum_tensor("e_ps_y", [P, 2, BANK], F32))

        w_loaded = [sem_(f"w_loaded{r}") for r in range(RING)]
        piece_done = sem_("piece_done")
        g_rows, s_rows = sem_("g_rows"), sem_("s_rows")
        gathered, scattered, held = io["gathered"], io["scattered"], io["held"]
        x_turned, xt_done = sem_("x_turned"), sem_("xt_done")
        silu_done, hid_done = sem_("silu_done"), sem_("hid_done")
        yt_done, y_turned, y_done = sem_("yt_done"), sem_("y_turned"), sem_("y_done")

        def source(e, s):
            name, q = (("w_gate_e", "w_up_e")[s % 2], s // 2) if s < 8 else ("w_down_e", s - 8)
            return io[name][bass.ds(layer * E + e, 1), :, q * CH:(q + 1) * CH].squeeze(0).rearrange("(k p) f -> p k f", p=P)

        def experts(eng, body):
            body(0, True, True)
            with eng.Fori(1, E - 1) as e:
                body(e, False, True)
            body(E - 1, False, False)

        with nc.Block() as block:
            @block.sync
            def _(sp):
                for s in range(RING):
                    sp.dma_start(w[:, s], source(0, s)).then_inc(w_loaded[s], 16)

                def body(e, first, more):
                    if more:
                        for s in range(NS):
                            sp.wait_ge(piece_done, e * NS + s + 1)
                            sp.sem_inc(held, 1)
                            sp.dma_start(w[:, s], source(e + 1, s)).then_inc(w_loaded[s], 16)
                experts(sp, body)

            @block.gpsimd
            def _(pool):
                def gather(e):
                    pool.wait_ge(x_turned, e * 4)
                    pool.sem_inc(held, 1)
                    nc.gpsimd.tensor_copy(ip_g[:], io["rows"][:, 0, bass.ds(e, 1)])
                    nc.gpsimd.tensor_copy(is_g[0:CAP_S], io["rows"][0:CAP_S, 1, bass.ds(e, 1)]).then_inc(g_rows, 1)
                    pool.wait_ge(g_rows, e + 1)
                    pool.sem_inc(held, 1)
                    nc.gpsimd.indirect_dma_start(xp[:], None, io["h"], bass.IndirectOffsetOnAxis(ap=ip_g[:, 0:1], axis=0)).then_inc(gathered, 16)
                    nc.gpsimd.indirect_dma_start(xs[:], None, io["h"], bass.IndirectOffsetOnAxis(ap=is_g[0:CAP_S, 0:1], axis=0)).then_inc(gathered, 16)

                def scatter(e):
                    pool.wait_ge(scattered, (layer * E + e) * 32)
                    pool.sem_inc(held, 1)
                    nc.gpsimd.tensor_copy(ip_s[:], io["rows"][:, 0, bass.ds(e, 1)])
                    nc.gpsimd.tensor_copy(is_s[0:CAP_S], io["rows"][0:CAP_S, 1, bass.ds(e, 1)]).then_inc(s_rows, 1)
                    pool.wait_ge(s_rows, e + 1)
                    pool.wait_ge(y_done, e * 4 + 4)
                    pool.sem_inc(held, 1)
                    nc.gpsimd.indirect_dma_start(io["y"], bass.IndirectOffsetOnAxis(ap=ip_s[:, 0:1], axis=0), yp[:], None, compute_op=ALU.add).then_inc(scattered, 16)
                    nc.gpsimd.indirect_dma_start(io["y"], bass.IndirectOffsetOnAxis(ap=is_s[0:CAP_S, 0:1], axis=0), ys[:], None, compute_op=ALU.add).then_inc(scattered, 16)

                gather(0)

                def body(e, first, more):
                    if more:
                        gather(e + 1)
                    scatter(e)
                experts(pool, body)
                pool.wait_ge(scattered, (layer + 1) * E * 32)
                pool.sem_inc(held, 1)

            @block.scalar
            def _(act):
                def x_part(e, g):
                    act.wait_ge(x_turned, e * 4 + g + 1)
                    act.activation(xt[:, 2 * g:2 * g + 2, :], ps_x[:, g % 2, 0:B2 * SLOTS].rearrange("p (k t) -> p k t", k=B2), ACT.Copy).then_inc(xt_done, 1)

                for g in range(4):
                    x_part(0, g)

                def body(e, first, more):
                    for s in range(NS):
                        out = ps_w[:, s % 4, 0:B2 * SLOTS].rearrange("p (k t) -> p k t", k=B2)
                        if s < 8 and s % 2 == 0:
                            act.wait_ge(piece_done, e * NS + s + 1)
                            act.wait_ge(hid_done, e * 4 + s // 2)
                            act.activation(gate[:], out, ACT.Silu).then_inc(silu_done, 1)
                        if s >= 8:
                            q = s - 8
                            act.wait_ge(piece_done, e * NS + s + 1)
                            if not first or q > 1:
                                act.wait_ge(y_turned, e * 4 + q - 1)
                            act.activation(yt[:, q % 2], out, ACT.Copy).then_inc(yt_done, 1)
                            if more and q < 2:
                                x_part(e + 1, 2 * q)
                                x_part(e + 1, 2 * q + 1)
                experts(act, body)

            @block.vector
            def _(dve):
                def y_part(e, q):
                    c = slice(q * CH, (q + 1) * CH)
                    dve.wait_ge(y_turned, e * 4 + q + 1)
                    if q == 0:
                        dve.wait_ge(scattered, (layer * E + e) * 32)
                    dve.tensor_scalar(yp[:, c], ps_y[:, q % 2, 0:CH], io["vals"][:, 0, bass.ds(e, 1)], None, ALU.mult)
                    dve.tensor_scalar(ys[:, c], ps_y[0:CAP_S, q % 2, CH:2 * CH], io["vals"][0:CAP_S, 1, bass.ds(e, 1)], None, ALU.mult).then_inc(y_done, 1)

                def body(e, first, more):
                    if not first:
                        y_part(e - 1, 3)
                    for q in range(4):
                        dve.wait_ge(piece_done, e * NS + 2 * q + 2)
                        dve.wait_ge(silu_done, e * 4 + q + 1)
                        dve.tensor_tensor(hid[:, 2 * q:2 * q + 2, :], ps_w[:, (2 * q + 1) % 4, 0:B2 * SLOTS].rearrange("p (k t) -> p k t", k=B2), gate[:], ALU.mult).then_inc(hid_done, 1)
                    for q in range(3):
                        y_part(e, q)
                experts(dve, body)
                y_part(E - 1, 3)

            @block.tensor
            def _(pe):
                def turn_x(e, g):
                    if g == 0:
                        pe.wait_ge(gathered, (layer * E + e) * 32 + 32)
                    if not isinstance(e, int) or e or g >= 2:
                        pe.wait_ge(xt_done, e * 4 + g - 1)
                    for k in range(B2):
                        c = slice((2 * g + k) * P, (2 * g + k + 1) * P)
                        pe.transpose(ps_x[:, g % 2, k * SLOTS:k * SLOTS + P], xp[:, c], io["ident"][:])
                        mm = pe.transpose(ps_x[:, g % 2, k * SLOTS + P:(k + 1) * SLOTS], xs[:, c], io["ident"][0:CAP_S, 0:CAP_S])
                    mm.then_inc(x_turned, 1)

                def turn_y(e, q):
                    pe.wait_ge(yt_done, e * 4 + q + 1)
                    if not isinstance(e, int) or e or q >= 2:
                        pe.wait_ge(y_done, e * 4 + q - 1)
                    for k in range(B2):
                        pe.transpose(ps_y[:, q % 2, k * P:(k + 1) * P], yt[:, q % 2, k, 0:P], io["ident"][:])
                        mm = pe.transpose(ps_y[0:CAP_S, q % 2, CH + k * P:CH + (k + 1) * P], yt[:, q % 2, k, P:SLOTS], io["ident"][:])
                    mm.then_inc(y_turned, 1)

                for g in range(4):
                    turn_x(0, g)

                def body(e, first, more):
                    for s in range(NS):
                        pe.wait_ge(w_loaded[s], e * 16 + 16)
                        if s == 0:
                            pe.wait_ge(xt_done, e * 4 + 4)
                        if s >= 4:
                            pe.wait_ge(hid_done, e * 4 + s // 2 - 1)
                        elif not first:
                            pe.wait_ge(yt_done, e * 4 - 3 + s)
                        groups = ((range(0, 6), 3), (range(6, 8), 4)) if s == 8 else ((range(KD), 0),)
                        for ks, need in groups:
                            if need:
                                pe.wait_ge(hid_done, e * 4 + need)
                            for m in range(B2):
                                for k in ks:
                                    mm = pe.matmul(ps_w[:, s % 4, m * SLOTS:(m + 1) * SLOTS], w[:, s, k, m * P:(m + 1) * P],
                                                   (xt if s < 8 else hid)[:, k, :], start=k == 0 and m == 0, stop=k == KD - 1, skip_group_check=True)
                        mm.then_inc(piece_done, 1)
                        if more and s in (8, 9):
                            turn_x(e + 1, 2 * (s - 8))
                            turn_x(e + 1, 2 * (s - 8) + 1)
                        if s == 0 and not first:
                            turn_y(e - 1, 3)
                        if s > 8:
                            turn_y(e, s - 9)
                experts(pe, body)
                turn_y(E - 1, 3)


def stage_embed(nc, sem, layer, io):
    KP = PLE // P
    RK = 2
    NR = KD // RK
    with ExitStack() as ctx:
        def sb(name, shape, dt=F32):
            return ctx.enter_context(nc.sbuf_tensor("g_" + name, shape, dt))

        def sem_(name):
            return sem("g_" + name)

        w_raw = sb("w_raw", [P, 2, RK, D])
        w_hi, w_lo = sb("w_hi", [P, KD + KP, D], F32R), sb("w_lo", [P, KD + KP, D], F32R)
        gain = sb("gain", [P, D])
        x, xn = sb("x", [P, 3, D]), sb("xn", [P, D])
        p = sb("p", [P, 2, PLE])
        at_hi, at_lo = sb("at_hi", [P, 2, KD + KP, P], F32R), sb("at_lo", [P, 2, KD + KP, P], F32R)
        gate, out = sb("gate", [P, 2, BANK]), sb("out", [P, 2, D])
        st = sb("st", [P, 16])
        ps_x = ctx.enter_context(nc.psum_tensor("g_ps_x", [P, KD, P], F32))
        ps_p = ctx.enter_context(nc.psum_tensor("g_ps_p", [P, BANK], F32))
        ps_g = ctx.enter_context(nc.psum_tensor("g_ps_g", [P, 2, BANK], F32))
        ps_e = ctx.enter_context(nc.psum_tensor("g_ps_e", [P, 2, BANK], F32))

        gain_loaded, w_hi_done, w_lo_done = sem_("gain_loaded"), sem_("w_hi_done"), sem_("w_lo_done")
        w_loaded = [sem_("w_loaded0"), sem_("w_loaded1")]
        x_loaded = [sem_("x_loaded0"), sem_("x_loaded1")]
        y_stored = [sem_("y_stored0"), sem_("y_stored1")]
        squared, rooted, normed, turned = (sem_(n) for n in ("squared", "rooted", "normed", "turned"))
        at_hi_done, at_lo_done, gate_mm, embed_mm = (sem_(n) for n in ("at_hi_done", "at_lo_done", "gate_mm", "embed_mm"))
        gated, y_done, norm_chain, out_chain = (sem_(n) for n in ("gated", "y_done", "norm_chain", "out_chain"))

        def tiles(eng, tile):
            with eng.Fori(0, TILES // 2 - 1) as j:
                for b in range(2):
                    tile(j * 2 + b, b, j, True)
            tile(TILES - 2, 0, TILES // 2 - 1, True)
            tile(TILES - 1, 1, TILES // 2 - 1, False)

        with nc.Block() as block:
            @block.sync
            def _(sp):
                def load(i, b):
                    if warm(i):
                        sp.wait_ge(y_done, i * 2 - 2)
                        sp.wait_ge(turned, i - 1)
                    sp.dma_start(x[:, b, :], io["y"][bass.ds(i * P, P), :]).then_inc(x_loaded[b], 16)
                    sp.dma_start(p[:, b, :], io["p"][bass.ds(layer * ROWS + i * P, P), :]).then_inc(x_loaded[b], 16)

                sp.dma_start(gain[:], io["ple_norm"][bass.ds(layer, 1), :].squeeze(0).partition_broadcast(P)).then_inc(gain_loaded, 16)
                load(0, 0)
                for n in range(NR + 1):
                    if n >= 2:
                        sp.wait_ge(w_lo_done, n - 1)
                    src = (io["w_ple_gate"][bass.ds(layer, 1), n * RK * P:(n + 1) * RK * P, :] if n < NR else io["w_ple_proj"][bass.ds(layer, 1)])
                    sp.dma_start(w_raw[:, n % 2], src.squeeze(0).rearrange("(k p) n -> p k n", p=P)).then_inc(w_loaded[n % 2], 16)

                def tile(i, b, j, more):
                    if more:
                        load(i + 1, 1 - b)
                    sp.wait_ge(y_done, i * 2 + 2)
                    sp.dma_start(io["y"][bass.ds(i * P, P), :], out[:, b, :]).then_inc(y_stored[b], 16)
                tiles(sp, tile)
                for s in y_stored:
                    sp.wait_ge(s, 16 * TILES // 2)

            @block.scalar
            def _(act):
                def prepare(i, b, j):
                    act.wait_ge(x_loaded[b], j * 32 + 32)
                    act.wait_ge(at_lo_done, i)
                    act.activation(ps_x[:].rearrange("p k t -> p (k t)"), x[:, b, :], ACT.Square, accum_out=st[:, b:b + 1]).then_inc(squared, 1)
                    act.wait_ge(squared, i + 1)
                    act.activation(st[:, 2 + b:3 + b], st[:, b:b + 1], ACT.Sqrt, bias=io["eps"][:, 0:1], scale=1.0 / D).then_inc(rooted, 1)

                def prepared(i, b):
                    act.wait_ge(turned, i + 1)
                    act.activation(at_hi[:, b, 0:KD, :], ps_x[:], ACT.Copy)
                    act.activation(at_hi[:, b, KD:KD + KP, :], ps_p[:, 0:KP * P].rearrange("p (k t) -> p k t", k=KP), ACT.Copy).then_inc(at_hi_done, 1)

                prepare(0, 0, 0)
                prepared(0, 0)
                for n in range(NR + 1):
                    act.wait_ge(w_loaded[n % 2], 16 * (n // 2 + 1))
                    act.activation(w_hi[:, n * RK:(n + 1) * RK, :], w_raw[:, n % 2], ACT.Copy).then_inc(w_hi_done, 1)

                def tile(i, b, j, more):
                    if more:
                        prepare(i + 1, 1 - b, j + b)
                    for c in range(2):
                        act.wait_ge(gate_mm, i * 2 + c + 1)
                        act.wait_ge(y_done, i * 2)
                        act.activation(gate[:, c, :], ps_g[:, c, :], ACT.Sigmoid).then_inc(gated, 1)
                    if more:
                        prepared(i + 1, 1 - b)
                tiles(act, tile)

            @block.vector
            def _(dve):
                def prepare(i, b, j):
                    dve.wait_ge(rooted, i + 1)
                    ch = Chain(dve, norm_chain, i, 1)
                    ch.link(dve.reciprocal(st[:, 4 + b:5 + b], st[:, 2 + b:3 + b]))
                    ch.close()
                    dve.wait_ge(turned, i)
                    dve.scalar_tensor_tensor(xn[:], x[:, b, :], st[:, 4 + b:5 + b], gain[:], ALU.mult, ALU.mult).then_inc(normed, 1)

                def prepared(i, b):
                    dve.wait_ge(at_hi_done, i + 1)
                    dve.tensor_tensor(at_lo[:, b, 0:KD, :], ps_x[:], at_hi[:, b, 0:KD, :].bitcast(F32), ALU.subtract)
                    dve.tensor_tensor(at_lo[:, b, KD:KD + KP, :], ps_p[:, 0:KP * P].rearrange("p (k t) -> p k t", k=KP),
                                      at_hi[:, b, KD:KD + KP, :].bitcast(F32), ALU.subtract).then_inc(at_lo_done, 1)

                dve.wait_ge(gain_loaded, 16)
                prepare(0, 0, 0)
                prepared(0, 0)
                for n in range(NR + 1):
                    dve.wait_ge(w_hi_done, n + 1)
                    dve.tensor_tensor(w_lo[:, n * RK:(n + 1) * RK, :], w_raw[:, n % 2], w_hi[:, n * RK:(n + 1) * RK, :].bitcast(F32), ALU.subtract).then_inc(w_lo_done, 1)

                def tile(i, b, j, more):
                    if more:
                        prepare(i + 1, 1 - b, j + b)
                        prepared(i + 1, 1 - b)
                    for c in range(2):
                        cs = slice(c * BANK, (c + 1) * BANK)
                        n = i * 2 + c
                        dve.wait_ge(gated, n + 1)
                        dve.wait_ge(embed_mm, n + 1)
                        if warm(i):
                            dve.wait_ge(y_stored[b], j * 16)
                        ch = Chain(dve, out_chain, n, 1)
                        ch.link(dve.tensor_tensor(out[:, b, cs], ps_e[:, c, :], gate[:, c, :], ALU.mult))
                        ch.close()
                        dve.tensor_tensor(out[:, b, cs], out[:, b, cs], x[:, b, cs], ALU.add).then_inc(y_done, 1)
                tiles(dve, tile)

            @block.tensor
            def _(pe):
                def turn(i, b):
                    pe.wait_ge(normed, i + 1)
                    for k in range(KD):
                        pe.transpose(ps_x[:, k, :], xn[:, k * P:(k + 1) * P], io["ident"][:])
                    for k in range(KP):
                        mm = pe.transpose(ps_p[:, k * P:(k + 1) * P], p[:, b, k * P:(k + 1) * P], io["ident"][:])
                    mm.then_inc(turned, 1)

                turn(0, 0)
                pe.wait_ge(w_lo_done, NR + 1)

                def tile(i, b, j, more):
                    pe.wait_ge(at_lo_done, i + 1)
                    for c in range(2):
                        cs = slice(c * BANK, (c + 1) * BANK)
                        pe.wait_ge(gated, i * 2)
                        for k in range(KD):
                            mm = split_matmul(pe, ps_g[:, c, :], (at_hi[:, b, k, :], at_lo[:, b, k, :]), (w_hi[:, k, cs], w_lo[:, k, cs]), k == 0, k == KD - 1)
                        mm.then_inc(gate_mm, 1)
                        if c == 0 and more:
                            turn(i + 1, 1 - b)
                    for c in range(2):
                        cs = slice(c * BANK, (c + 1) * BANK)
                        pe.wait_ge(y_done, i * 2)
                        for k in range(KD, KD + KP):
                            mm = split_matmul(pe, ps_e[:, c, :], (at_hi[:, b, k, :], at_lo[:, b, k, :]), (w_hi[:, k, cs], w_lo[:, k, cs]), k == KD, k == KD + KP - 1)
                        mm.then_inc(embed_mm, 1)
                tiles(pe, tile)


@contextmanager
def counted(nc):
    with ExitStack() as ctx:
        sems = []

        def sem(name):
            sems.append(ctx.enter_context(nc.semaphore(name)))
            return sems[-1]

        yield sem
        numbers = sorted(s.num for s in sems)
        starts = [n for n in numbers if n - 1 not in numbers]
        ends = [n + 1 for n in numbers if n + 1 not in numbers]
        with nc.Block() as block:
            @block.sync
            def _(sp):
                for start, end in zip(starts, ends):
                    sp.sem_clear(range(start, end))


def encoder(nc, io):
    io = dict(io)
    io["w_gate_e"], io["w_up_e"], io["w_down_e"] = (io[n].rearrange("l e d f -> (l e) d f") for n in ("w_gate_e", "w_up_e", "w_down_e"))
    io["qkT"] = nc.dram_tensor("qkT", [NQK, P, ROWS], F32, kind="Internal").ap()
    io["v"] = nc.dram_tensor("v", [ROWS, V_W], F32, kind="Internal").ap()
    io["h"] = nc.dram_tensor("h", [ROWS, D], F32, kind="Internal").ap()
    with ExitStack() as ctx:
        ident = ctx.enter_context(nc.sbuf_tensor("ident", [P, P], F32))
        small = ctx.enter_context(nc.sbuf_tensor("small", [P, 8], F32))
        logits = ctx.enter_context(nc.sbuf_tensor("logits", [P, TILES, E], F32))
        vals = ctx.enter_context(nc.sbuf_tensor("vals", [P, 2, E], F32))
        rows = ctx.enter_context(nc.sbuf_tensor("rows", [P, 2, E], U32))
        start_loaded = ctx.enter_context(nc.semaphore("start_loaded"))
        own = {n: ctx.enter_context(nc.semaphore(n)) for n in ("gathered", "scattered", "held")}
        io.update(own)
        io.update(ident=ident, logits=logits, vals=vals, rows=rows, eps=small[:, 4:5], lam_init=small[:, 0:2], lam_rest=small[:, 2:4])

        with nc.Block() as block:
            @block.sync
            def _(sp):
                sp.dma_start(ident[:], io["ident_in"]).then_inc(start_loaded, 16)
                sp.dma_start(small[:], io["small_in"]).then_inc(start_loaded, 16)
                sp.dma_start(io["y"], io["x"]).then_inc(start_loaded, 16)
                sp.wait_ge(start_loaded, 48)

        with nc.Fori(0, DEPTH) as layer:
            with counted(nc) as sem:
                stage_project(nc, sem, layer, io)
            with nc.sbuf_tensor("mix", [P, TILES, D], F32) as mix:
                io["mix"] = mix
                with counted(nc) as sem:
                    stage_dense(nc, sem, layer, io, 0, PROMPT)
                    stage_dense(nc, sem, layer, io, PROMPT, SAMPLE)
                    stage_window(nc, sem, layer, io)
                with counted(nc) as sem:
                    stage_mix(nc, sem, layer, io)
                    stage_choose(nc, sem, io)
            with counted(nc) as sem:
                stage_experts(nc, sem, layer, io)
                stage_embed(nc, sem, layer, io)


def constants():
    inv = np.float32(10000.0) ** (-np.arange(0, HD, 2, dtype=np.float32) / np.float32(HD))
    pos = np.concatenate([np.arange(PROMPT), np.arange(SAMPLE)]).astype(np.float32)
    ang = pos[:, None] * inv[None, :].astype(np.float32)
    cos, sin = np.cos(ang), np.sin(ang)
    trig = np.concatenate([cos, cos, -sin, sin], axis=1).astype(np.float32)
    masks = np.zeros((2, TILES, P, P), np.float32)
    q, k = np.arange(P)[:, None], np.arange(P)[None, :]
    masks[0][:, (k < q)] = MASKED / SCALE
    masks[1][:, (k > q)] = MASKED / SCALE
    masks[0, [0, PROMPT // P]] = MASKED / SCALE
    masks[1, [PROMPT // P - 1, TILES - 1]] = MASKED / SCALE
    small = np.zeros((P, 8), np.float32)
    for i in range(DEPTH):
        lam_init = 0.8 - 0.6 * math.exp(-0.3 * i)
        small[:, i] = lam_init
        small[:, 2 + i] = 1.0 - lam_init
    small[:, 4] = EPS
    return trig, masks, small


def kernel(**inputs):
    import ml_dtypes
    import concourse.bacc as bacc
    from concourse.bass_utils import run_bass_kernel_spmd

    def rows_of(a, b):
        return np.concatenate([np.asarray(a), np.asarray(b)], axis=-2)

    trig, masks, small = constants()
    given = {n: np.ascontiguousarray(v) for n, v in inputs.items() if n not in ("x_prompt", "x_sample", "p_prompt", "p_sample")}
    given["x"] = rows_of(inputs["x_prompt"], inputs["x_sample"]).reshape(ROWS, D)
    given["p"] = rows_of(inputs["p_prompt"], inputs["p_sample"]).reshape(DEPTH * ROWS, PLE)
    given.update(trig=trig, masks=masks.astype(ml_dtypes.bfloat16), small_in=small,
                 ident_in=np.eye(P, dtype=np.float32), identb=np.eye(P, dtype=ml_dtypes.bfloat16))
    nc = bacc.Bacc("TRN2", target_bir_lowering=False, num_devices=1)
    io = {n: nc.dram_tensor(f"in_{n}", a.shape, mybir.dt.from_np(a.dtype), kind="ExternalInput").ap() for n, a in given.items()}
    io["y"] = nc.dram_tensor("y", (ROWS, D), F32, kind="ExternalOutput").ap()
    encoder(nc, io)
    r = run_bass_kernel_spmd(nc, [{f"in_{n}": a for n, a in given.items()}], core_ids=[0])
    y = r.results[0]["y"]
    return y[:PROMPT].reshape(1, PROMPT, D), y[PROMPT:].reshape(1, SAMPLE, D)
```

```python
import math
from contextlib import ExitStack, contextmanager

import numpy as np

import concourse.bass as bass
from concourse import mybir

ALU = mybir.AluOpType
ACT = mybir.ActivationFunctionType
AX_X = mybir.AxisListType.X
F32 = mybir.dt.float32
F32R = mybir.dt.float32r
BF16 = mybir.dt.bfloat16
U32 = mybir.dt.uint32

P = 128
D = 1024
KD = D // P
DEPTH = 2
PROMPT, SAMPLE = 1024, 256
ROWS = PROMPT + SAMPLE
TILES = ROWS // P
HD = 64
HALF = HD // 2
DA_HEADS, SW_KV, GROUP = 4, 2, 4
NQK = 13
V_W = 640
D_IN = 2304
E = 16
CAP_P, CAP_S = 2 * PROMPT // E, 2 * SAMPLE // E
SLOTS = CAP_P + CAP_S
PLE = 256
EPS = 1e-6
SCALE = HD ** -0.5
MASKED = -1e30
BANK = 512


class Chain:

    def __init__(self, eng, sem, tile, per):
        self.eng, self.sem, self.base, self.per, self.n = eng, sem, tile * per, per, 0

    def link(self, ins):
        ins.then_inc(self.sem, 1)
        self.n += 1
        self.eng.wait_ge(self.sem, self.base + self.n)

    def close(self):
        assert self.n == self.per, (self.sem.name, self.n)


def paired(eng, count, lag, step):
    for i in range(4):
        step(i, i % 2, lambda k, i=i: 0 <= i - k < count, i // 2)
    with eng.Fori(2, count // 2) as j:
        for b in range(2):
            step(j * 2 + b, b, lambda k: True, j)
    for i in range(count, count + lag):
        step(i, i % 2, lambda k, i=i: 0 <= i - k < count, i // 2)


def tiles(eng, tile):
    tile(0, 0, 0, True)
    tile(1, 1, 0, True)
    with eng.Fori(1, TILES // 2 - 1) as j:
        for b in range(2):
            tile(j * 2 + b, b, j, True)
    tile(TILES - 2, 0, TILES // 2 - 1, True)
    tile(TILES - 1, 1, TILES // 2 - 1, False)


def warm(i):
    return not isinstance(i, int) or i >= 2


def split_matmul(pe, out, a, b, first=True, last=True):
    pe.matmul(out, a[0], b[0], start=first, stop=False)
    pe.matmul(out, a[0], b[1], start=False, stop=False)
    return pe.matmul(out, a[1], b[0], start=False, stop=last)


def over(ap, count):
    w = ap.shape[-1]
    return ap.rearrange("p (a w) -> p a w", a=1).to_broadcast([ap.shape[0], count, w])


def along(ap, width):
    n = ap.shape[-1]
    return ap.rearrange("p (n a) -> p n a", a=1).to_broadcast([ap.shape[0], n, width])


def stage_project(nc, sem, layer, io):
    CH = 256
    NP = D_IN // CH
    CHUNKS = [(0, 8, 0, 0, None), (512, 8, 1, 4, None), (1536, 8, 2, 8, None), (2048, 2, 3, 12, 512),
              (1024, 0, None, None, 0)]
    NCH = len(CHUNKS)
    SPLIT_BY = (2, 4, 6, 7, NP)
    pieces = [c // CH + j for c, *_ in CHUNKS for j in range(2 if c != 2048 else 1)]
    with ExitStack() as ctx:
        def sb(name, shape, dt=F32):
            return ctx.enter_context(nc.sbuf_tensor(name, shape, dt))

        w_raw = sb("p_w_raw", [P, 2, KD, CH])
        w_hi = sb("p_w_hi", [P, KD, D_IN], F32R)
        w_lo = sb("p_w_lo", [P, KD, D_IN], F32R)
        x_in = sb("p_x", [P, 2, D])
        gain_x = sb("p_gain_x", [P, D])
        gains = sb("p_gains", [P, 4, HD])
        trig = sb("p_trig", [P, 2, 2, HD])
        cosg = sb("p_cosg", [P, 4, HD])
        sing = sb("p_sing", [P, 4, HD])
        ht_hi = sb("p_ht_hi", [P, 2, KD, P], F32R)
        ht_lo = sb("p_ht_lo", [P, 2, KD, P], F32R)
        qn = sb("p_qn", [P, 512])
        rot = sb("p_rot", [P, 512])
        qr = sb("p_qr", [P, 512])
        qk_st = sb("p_qk_st", [P, 2, 512])
        v_st = sb("p_v_st", [P, 512])
        vb_st = sb("p_vb_st", [P, P])
        st = sb("p_st", [P, 64])
        ps_mm = ctx.enter_context(nc.psum_tensor("p_ps_mm", [P, 2, BANK], F32))
        ps_t = ctx.enter_context(nc.psum_tensor("p_ps_t", [P, 2, BANK], F32))
        ps_x = ctx.enter_context(nc.psum_tensor("p_ps_x", [P, KD, P], F32))
        sq = ctx.enter_context(nc.psum_tensor("p_ps_sq", [P, BANK], F32))

        w_loaded = [sem("p_w_loaded0"), sem("p_w_loaded1")]
        x_loaded = [sem("p_x_loaded0"), sem("p_x_loaded1")]
        trig_loaded = [sem("p_trig_loaded0"), sem("p_trig_loaded1")]
        gain_x_loaded, gains_loaded = sem("p_gain_x_loaded"), sem("p_gains_loaded")
        w_hi_done, w_lo_done = sem("p_w_hi_done"), sem("p_w_lo_done")
        x_squared, x_rms, x_normed, x_turned = (sem(f"p_x_{n}") for n in ("squared", "rms", "normed", "turned"))
        ht_hi_done, ht_lo_done = sem("p_ht_hi_done"), sem("p_ht_lo_done")
        tables_done, projected = sem("p_tables_done"), sem("p_projected")
        q_squared, q_summed, q_rms, q_scaled = (sem(f"p_q_{n}") for n in ("squared", "summed", "rms", "scaled"))
        q_roped, q_turned, q_staged = (sem(f"p_q_{n}") for n in ("roped", "turned", "staged"))
        q_stored = [sem("p_q_stored0"), sem("p_q_stored1")]
        v_stored, vb_copied, vb_stored = sem("p_v_stored"), sem("p_vb_copied"), sem("p_vb_stored")
        norm_chain, rope_chain = sem("p_norm_chain"), sem("p_rope_chain")
        va_copied = sem("p_va_copied")

        ssq, rms, rstd = st[:, 0:2], st[:, 2:4], st[:, 4:6]
        q_ssq, q_rt, q_rs = st[:, 16:24], st[:, 24:32], st[:, 32:40]
        w_src = io["w_in"].rearrange("l (k p) n -> p l k n", p=P)

        def bank(b, c):
            return (NCH * b + c) % 2

        with nc.Block() as block:
            @block.sync
            def _(sp):
                sp.dma_start(gain_x[:], io["attn_norm"][bass.ds(layer, 1), :].squeeze(0).partition_broadcast(P)).then_inc(gain_x_loaded, 16)

                def load_x(i, b):
                    if warm(i):
                        sp.wait_ge(x_turned, i - 1)
                        sp.wait_ge(tables_done, i - 1)
                    sp.dma_start(x_in[:, b, :], io["y"][bass.ds(i * P, P), :]).then_inc(x_loaded[b], 16)
                    sp.dma_start(trig[:, b, :, :], io["trig"][bass.ds(i * P, P), :].rearrange("p (t d) -> p t d", t=2)).then_inc(trig_loaded[b], 16)

                load_x(0, 0)
                for n, pc in enumerate(pieces):
                    if n == 1:
                        for g, name in enumerate(("q_norm_a", "k_norm_a", "q_norm_b", "k_norm_b")):
                            sp.dma_start(gains[:, g, :], io[name][bass.ds(layer, 1), :].squeeze(0).partition_broadcast(P)).then_inc(gains_loaded, 16)
                    if n == 2:
                        load_x(1, 1)
                    if n >= 2:
                        sp.wait_ge(w_lo_done, n - 1)
                    sp.dma_start(w_raw[:, n % 2], w_src[:, bass.ds(layer, 1), :, pc * CH:(pc + 1) * CH].squeeze(1)).then_inc(w_loaded[n % 2], 16)

                def tile(i, b, j, more):
                    if more and warm(i + 1):
                        load_x(i + 1, 1 - b)
                    for c, (_, heads, _, blk, vcol) in enumerate(CHUNKS):
                        if heads:
                            nb = heads // 2
                            sp.wait_ge(q_staged, i * 4 + c + 1)
                            sp.sem_inc(io["held"], 1)
                            sp.dma_start(io["qkT"][blk:blk + nb, :, bass.ds(i * P, P)].rearrange("c p t -> p c t"),
                                         qk_st[:, c % 2, 0:nb * P].rearrange("p (c t) -> p c t", c=nb)).then_inc(q_stored[c % 2], 16)
                        if vcol == 512:
                            sp.wait_ge(vb_copied, i + 1)
                            sp.dma_start(io["v"][bass.ds(i * P, P), 512:640], vb_st[:]).then_inc(vb_stored, 16)
                        if vcol == 0:
                            sp.wait_ge(va_copied, i + 1)
                            sp.sem_inc(io["held"], 1)
                            sp.dma_start(io["v"][bass.ds(i * P, P), 0:512], v_st[:]).then_inc(v_stored, 16)
                tiles(sp, tile)
                for s in q_stored:
                    sp.wait_ge(s, 32 * TILES)
                sp.wait_ge(vb_stored, 16 * TILES)
                sp.wait_ge(v_stored, 16 * TILES)

            @block.scalar
            def _(act):
                def prepare(i, b, j):
                    act.wait_ge(x_loaded[b], j * 16 + 16)
                    act.wait_ge(ht_lo_done, i)
                    act.activation(ps_x[:].rearrange("p k t -> p (k t)"), x_in[:, b, :], ACT.Square, accum_out=ssq[:, b:b + 1]).then_inc(x_squared, 1)
                    act.wait_ge(x_squared, i + 1)
                    act.activation(rms[:, b:b + 1], ssq[:, b:b + 1], ACT.Sqrt, bias=io["eps"][:, 0:1], scale=1.0 / D).then_inc(x_rms, 1)

                def prepared(i, b):
                    act.wait_ge(x_turned, i + 1)
                    act.activation(ht_hi[:, b], ps_x[:], ACT.Copy).then_inc(ht_hi_done, 1)

                def split(n, pc):
                    act.wait_ge(w_loaded[n % 2], 16 * (n // 2 + 1))
                    act.activation(w_hi[:, :, pc * CH:(pc + 1) * CH], w_raw[:, n % 2], ACT.Copy).then_inc(w_hi_done, 1)

                prepare(0, 0, 0)
                split(0, pieces[0])
                prepared(0, 0)

                def split_for(c):
                    for n in range(max(SPLIT_BY[c - 1] if c else 0, 1), SPLIT_BY[c]):
                        split(n, pieces[n])
                split_for(0)

                def stage_out(i, b, c):
                    nb = CHUNKS[c][1] // 2
                    act.wait_ge(q_turned, i * 4 + c + 1)
                    act.wait_ge(q_stored[c % 2], i * 32 + 16 * (c // 2))
                    act.activation(qk_st[:, c % 2, 0:nb * P], ps_t[:, c % 2, 0:nb * P], ACT.Copy).then_inc(q_staged, 1)

                def tile(i, b, j, more):
                    for c, (_, heads, _, _, vcol) in enumerate(CHUNKS):
                        if isinstance(i, int) and i == 0 and c + 1 < NCH:
                            split_for(c + 1)
                        act.wait_ge(projected, i * NCH + c + 1)
                        ps = ps_mm[:, bank(b, c), :]
                        if heads:
                            act.wait_ge(q_summed, i * 4 + c)
                            act.activation(sq[:, 0:heads * HD], ps[:, 0:heads * HD], ACT.Square).then_inc(q_squared, 1)
                            act.wait_ge(q_summed, i * 4 + c + 1)
                            act.activation(q_rt[:, 0:heads], q_ssq[:, 0:heads], ACT.Sqrt, bias=io["eps"][:, 0:1], scale=1.0 / HD).then_inc(q_rms, 1)
                        if vcol == 0:
                            act.wait_ge(v_stored, i * 16)
                            act.activation(v_st[:], ps, ACT.Copy).then_inc(va_copied, 1)
                        if c:
                            stage_out(i, b, c - 1)
                        if c == 1 and more:
                            prepare(i + 1, 1 - b, j + b)
                        if c == 3 and more:
                            prepared(i + 1, 1 - b)
                tiles(act, tile)

            @block.vector
            def _(dve):
                dve.wait_ge(gain_x_loaded, 16)

                def prepare(i, b, j):
                    dve.wait_ge(x_rms, i + 1)
                    ch = Chain(dve, norm_chain, i, 1)
                    ch.link(dve.reciprocal(rstd[:, b:b + 1], rms[:, b:b + 1]))
                    ch.close()
                    dve.scalar_tensor_tensor(x_in[:, b, :], x_in[:, b, :], rstd[:, b:b + 1], gain_x[:], ALU.mult, ALU.mult).then_inc(x_normed, 1)

                def prepared(i, b):
                    dve.wait_ge(ht_hi_done, i + 1)
                    dve.tensor_tensor(ht_lo[:, b], ps_x[:], ht_hi[:, b].bitcast(F32), ALU.subtract).then_inc(ht_lo_done, 1)

                def split(n, pc):
                    dve.wait_ge(w_hi_done, n + 1)
                    c0 = pc * CH
                    dve.tensor_tensor(w_lo[:, :, c0:c0 + CH], w_raw[:, n % 2], w_hi[:, :, c0:c0 + CH].bitcast(F32), ALU.subtract).then_inc(w_lo_done, 1)

                prepare(0, 0, 0)
                split(0, pieces[0])
                prepared(0, 0)

                def split_for(c):
                    for n in range(max(SPLIT_BY[c - 1] if c else 0, 1), SPLIT_BY[c]):
                        split(n, pieces[n])
                split_for(0)
                dve.wait_ge(gains_loaded, 16 * 4)

                def tile(i, b, j, more):
                    dve.wait_ge(trig_loaded[b], j * 16 + 16)
                    dve.wait_ge(q_roped, i * 4)
                    dve.tensor_tensor(cosg[:], gains[:], over(trig[:, b, 0, :], 4), ALU.mult)
                    dve.tensor_tensor(sing[:, :, 0:HALF], gains[:, :, HALF:HD], over(trig[:, b, 1, 0:HALF], 4), ALU.mult)
                    ch = Chain(dve, tables_done, i, 1)
                    ch.link(dve.tensor_tensor(sing[:, :, HALF:HD], gains[:, :, 0:HALF], over(trig[:, b, 1, HALF:HD], 4), ALU.mult))
                    for c, (_, heads, g, _, vcol) in enumerate(CHUNKS):
                        if isinstance(i, int) and i == 0 and c + 1 < NCH:
                            split_for(c + 1)
                        if heads:
                            w = heads * HD
                            ps = ps_mm[:, bank(b, c), 0:w].rearrange("p (h d) -> p h d", d=HD)
                            qnv, rotv, qrv = (t[:, 0:w].rearrange("p (h d) -> p h d", d=HD) for t in (qn, rot, qr))
                            n = i * 4 + c
                            dve.wait_ge(q_squared, n + 1)
                            dve.tensor_reduce(q_ssq[:, 0:heads], sq[:, 0:w].rearrange("p (h d) -> p h d", d=HD), AX_X, ALU.add).then_inc(q_summed, 1)
                            dve.wait_ge(q_rms, n + 1)
                            ch = Chain(dve, rope_chain, n, 2)
                            ch.link(dve.reciprocal(q_rs[:, 0:heads], q_rt[:, 0:heads]))
                            dve.tensor_tensor(qnv, ps, along(q_rs[:, 0:heads], HD), ALU.mult).then_inc(q_scaled, 1)
                            if vcol == 512:
                                dve.wait_ge(vb_stored, i * 16)
                                dve.tensor_copy(vb_st[:], ps_mm[:, bank(b, c), P:2 * P]).then_inc(vb_copied, 1)
                            dve.wait_ge(q_scaled, n + 1)
                            dve.wait_ge(q_turned, n)
                            dve.tensor_tensor(qrv, qnv, over(cosg[:, g, :], heads), ALU.mult)
                            dve.tensor_tensor(rotv[:, :, 0:HALF], qnv[:, :, HALF:HD], over(sing[:, g, 0:HALF], heads), ALU.mult)
                            ch.link(dve.tensor_tensor(rotv[:, :, HALF:HD], qnv[:, :, 0:HALF], over(sing[:, g, HALF:HD], heads), ALU.mult))
                            ch.close()
                            dve.tensor_tensor(qrv, qrv, rotv, ALU.add).then_inc(q_roped, 1)
                        if c == 1 and more:
                            prepare(i + 1, 1 - b, j + b)
                        if c == 3 and more:
                            prepared(i + 1, 1 - b)
                tiles(dve, tile)

            @block.tensor
            def _(pe):
                def turn_x(i, b):
                    pe.wait_ge(x_normed, i + 1)
                    for k in range(KD):
                        mm = pe.transpose(ps_x[:, k, :], x_in[:, b, k * P:(k + 1) * P], io["ident"][:])
                    mm.then_inc(x_turned, 1)

                def turn_q(i, c):
                    nb = CHUNKS[c][1] // 2
                    pe.wait_ge(q_roped, i * 4 + c + 1)
                    pe.wait_ge(q_staged, i * 4 + max(c - 1, 0))
                    for k in range(nb):
                        mm = pe.transpose(ps_t[:, c % 2, k * P:(k + 1) * P], qr[:, k * P:(k + 1) * P], io["ident"][:])
                    mm.then_inc(q_turned, 1)

                turn_x(0, 0)

                def tile(i, b, j, more):
                    pe.wait_ge(ht_lo_done, i + 1)
                    for c, (c0, heads, _, _, vcol) in enumerate(CHUNKS):
                        w = 256 if vcol == 512 else 512
                        pe.wait_ge(w_lo_done, SPLIT_BY[c])
                        if c == 0:
                            pe.wait_ge(q_scaled, i * 4)
                            pe.wait_ge(vb_copied, i)
                        elif c == 1:
                            pe.wait_ge(va_copied, i)
                        else:
                            pe.wait_ge(q_scaled, i * 4 + c - 1)
                        ps = ps_mm[:, bank(b, c), 0:w]
                        for k in range(KD):
                            mm = split_matmul(pe, ps, (ht_hi[:, b, k, :], ht_lo[:, b, k, :]),
                                              (w_hi[:, k, c0:c0 + w], w_lo[:, k, c0:c0 + w]), k == 0, k == KD - 1)
                        mm.then_inc(projected, 1)
                        if c:
                            turn_q(i, c - 1)
                        if c == 2 and more:
                            turn_x(i + 1, 1 - b)
                tiles(pe, tile)


def stage_dense(nc, sem, layer, io, off, S):
    T, KB = S // P, S // P
    N = DA_HEADS * T
    CW = min(S, BANK)
    tag = f"d{off}_"
    with ExitStack() as ctx:
        def sb(name, shape, dt=F32):
            return ctx.enter_context(nc.sbuf_tensor(tag + name, shape, dt))

        def sem_(name):
            return sem(tag + name)

        k_raw = sb("k_raw", [P, S])
        k_hi, k_lo = sb("k_hi", [P, S], F32R), sb("k_lo", [P, S], F32R)
        v = sb("v", [P, DA_HEADS, KB, P])
        q_raw = sb("q_raw", [P, 2, P])
        q_hi, q_lo = sb("q_hi", [P, 2, P], F32R), sb("q_lo", [P, 2, P], F32R)
        e = sb("e", [P, 2, 2, S])
        at = sb("at", [P, KB, P])
        st = sb("st", [P, 32])
        lam_v = sb("lam_v", [P, 4, HD])
        lam = sb("lam", [P, 8])
        ps_s = ctx.enter_context(nc.psum_tensor(tag + "ps_s", [P, 2, 1024], F32))
        ps_t = ctx.enter_context(nc.psum_tensor(tag + "ps_t", [P, 8, P], F32))
        ps_o = ctx.enter_context(nc.psum_tensor(tag + "ps_o", [P, 2, BANK], F32))

        q_loaded = [sem_("q_loaded0"), sem_("q_loaded1")]
        k_loaded, v_loaded, k_split = (sem_(n) for n in ("k_loaded", "v_loaded", "k_split"))
        k_hi_done, q_hi_done, q_lo_done = (sem_(n) for n in ("k_hi_done", "q_hi_done", "q_lo_done"))
        scored, max_done, exp_done = sem_("scored"), sem_("max_done"), sem_("exp_done")
        coef_done, combined, turned = sem_("coef_done"), sem_("combined"), sem_("turned")
        at_done, valued, stored = (sem_(n) for n in ("at_done", "valued", "stored"))
        max_chain, coef_chain = sem_("max_chain"), sem_("coef_chain")
        lam_loaded, lam_dots, lam_exps, lam_chain = (sem_(n) for n in ("lam_loaded", "lam_dots", "lam_exps", "lam_chain"))

        def mx(b):
            return st[:, 2 * b:2 * b + 2]

        def neg_max(b):
            return st[:, 4 + 2 * b:6 + 2 * b]

        def sums(b):
            return st[:, 8 + 2 * b:10 + 2 * b]

        def inv(b):
            return st[:, 12 + 2 * b:14 + 2 * b]

        def coef(b):
            return st[:, 16 + b:17 + b]

        def steps(eng, step):
            if T % 2 or DA_HEADS * T <= 8:
                for n in range(N + 3):
                    step(n // T, n % T, n, lambda k, n=n: 0 <= n - k < N)
                return
            for t in range(T):
                step(0, t, t, lambda k, t=t: t - k >= 0)
            with eng.Fori(1, DA_HEADS) as h:
                for t in range(T):
                    step(h, t, h * T + t, lambda k: True)
            for t in range(3):
                step(DA_HEADS, t, N + t, lambda k, t=t: t - k < 0)

        def back(h, t, k):
            n = t - k
            return (h, n) if n >= 0 else ((h - 1, n + T) if n + T >= 0 else (h - 2, n + 2 * T))

        with nc.Block() as block:
            @block.sync
            def _(sp):
                for r, name in enumerate(("lambda_q1", "lambda_k1", "lambda_q2", "lambda_k2")):
                    sp.dma_start(lam_v[:, r, :], io[name][bass.ds(layer, 1), :].squeeze(0).partition_broadcast(P)).then_inc(lam_loaded, 16)

                def load_q(h, t, n):
                    if warm(n):
                        sp.wait_ge(q_lo_done, n - 1)
                    sp.dma_start(q_raw[:, t % 2, :], io["qkT"][bass.ds(h, 1), :, off + t * P:off + (t + 1) * P].squeeze(0)).then_inc(q_loaded[t % 2], 16)

                def step(h, t, n, on):
                    if on(0) and t == 0:
                        sp.wait_ge(k_split, h)
                        sp.dma_start(k_raw[:], io["qkT"][bass.ds(h + 4, 1), :, off:off + S].squeeze(0)).then_inc(k_loaded, 16)
                    if on(0):
                        load_q(h, t, n)
                    if isinstance(n, int) and n == 1:
                        for k in range(KB):
                            sp.dma_start(v[:, :, k, :], io["v"][off + k * P:off + (k + 1) * P, 0:DA_HEADS * P].rearrange("p (h d) -> p h d", d=P)).then_inc(v_loaded, 16)
                steps(sp, step)

            @block.scalar
            def _(act):
                act.wait_ge(lam_dots, 1)
                act.activation(lam[:, 2:4], lam[:, 0:2], ACT.Exp).then_inc(lam_exps, 1)

                def split_q(h, t, n):
                    act.wait_ge(q_loaded[t % 2], h * (8 * T) + (t // 2) * 16 + 16)
                    if warm(n):
                        act.wait_ge(scored, n * 2 - 2)
                    act.activation(q_hi[:, t % 2, :], q_raw[:, t % 2, :], ACT.Copy).then_inc(q_hi_done, 1)

                def step(h, t, n, on):
                    b = t % 2
                    if on(0) and t == 0:
                        act.wait_ge(k_loaded, h * 16 + 16)
                        act.wait_ge(scored, h * T * 2)
                        act.activation(k_hi[:], k_raw[:], ACT.Copy).then_inc(k_hi_done, 1)
                        split_q(h, 0, n)
                    if on(0) and t + 1 < T:
                        split_q(h, t + 1, n + 1)
                    if on(2):
                        act.wait_ge(turned, n - 1)
                        act.activation(at[:], ps_t[:, 0:KB, :], ACT.Copy).then_inc(at_done, 1)
                    if on(0):
                        for c in range(2):
                            act.wait_ge(max_done, n * 2 + c + 1)
                            if warm(n):
                                act.wait_ge(turned, n - 1)
                                act.wait_ge(combined, n - 1)
                            act.activation(e[:, b, c, :], ps_s[:, c, 0:S], ACT.Exp, bias=neg_max(b)[:, c:c + 1],
                                           scale=SCALE, accum_out=sums(b)[:, c:c + 1]).then_inc(exp_done, 1)
                steps(act, step)

            @block.vector
            def _(dve):
                dve.wait_ge(lam_loaded, 64)
                ch = Chain(dve, lam_chain, 0, 4)
                pairs = lam_v[:].rearrange("p (a b) d -> p a b d", b=2)
                ch.link(dve.tensor_tensor(pairs[:, :, 0, :], pairs[:, :, 0, :], pairs[:, :, 1, :], ALU.mult))
                dve.tensor_reduce(lam[:, 0:2], pairs[:, :, 0, :], AX_X, ALU.add).then_inc(lam_dots, 1)
                dve.wait_ge(lam_exps, 1)
                ch.link(dve.tensor_tensor(lam[:, 4:5], lam[:, 3:4], lam[:, 2:3], ALU.subtract))
                ch.link(dve.tensor_scalar(lam[:, 6:7], io["lam_init"][:, bass.ds(layer, 1)], -1.0, None, ALU.mult))
                ch.link(dve.tensor_tensor(lam[:, 5:6], lam[:, 4:5], lam[:, 6:7], ALU.add))
                ch.close()

                def split_q(b, n):
                    dve.wait_ge(q_hi_done, n + 1)
                    dve.tensor_tensor(q_lo[:, b, :], q_raw[:, b, :], q_hi[:, b, :].bitcast(F32), ALU.subtract).then_inc(q_lo_done, 1)

                def maximum(b, n, c):
                    dve.wait_ge(scored, n * 2 + c + 1)
                    ch = Chain(dve, max_chain, n * 2 + c, 1)
                    ch.link(dve.tensor_reduce(mx(b)[:, c:c + 1], ps_s[:, c, 0:S], AX_X, ALU.max))
                    ch.close()
                    dve.tensor_scalar(neg_max(b)[:, c:c + 1], mx(b)[:, c:c + 1], -SCALE, None, ALU.mult).then_inc(max_done, 1)

                def step(h, t, n, on):
                    b = t % 2
                    if on(0) and t == 0:
                        dve.wait_ge(k_hi_done, h + 1)
                        dve.tensor_tensor(k_lo[:], k_raw[:], k_hi[:].bitcast(F32), ALU.subtract).then_inc(k_split, 1)
                        split_q(b, n)
                    if on(0):
                        maximum(b, n, 0)
                        if t + 1 < T:
                            split_q(1 - b, n + 1)
                    if on(3):
                        hb, tb = back(h, t, 3)
                        dve.wait_ge(valued, n - 2)
                        dve.tensor_scalar(io["mix"][:, off // P + tb, bass.ds(hb * P, P)], ps_o[:, (tb % 2), 0:P], inv(tb % 2)[:, 0:1], None, ALU.mult).then_inc(stored, 1)
                    if on(1):
                        b1 = 1 - b
                        dve.wait_ge(exp_done, n * 2)
                        if on(3):
                            dve.wait_ge(stored, n - 2)
                        ch = Chain(dve, coef_chain, n - 1, 1)
                        ch.link(dve.reciprocal(inv(b1), sums(b1)))
                        ch.close()
                        dve.scalar_tensor_tensor(coef(b1), sums(b1)[:, 0:1], lam[:, 5:6], inv(b1)[:, 1:2], ALU.mult, ALU.mult).then_inc(coef_done, 1)
                        dve.wait_ge(coef_done, n)
                        dve.scalar_tensor_tensor(e[:, b1, 0, :], e[:, b1, 1, :], coef(b1), e[:, b1, 0, :], ALU.mult, ALU.add).then_inc(combined, 1)
                    if on(0):
                        maximum(b, n, 1)
                steps(dve, step)

            @block.tensor
            def _(pe):
                def scores(b, n, c, used):
                    if used:
                        pe.wait_ge(exp_done, n * 2 - 1 + c)
                    rows = slice(c * HD, (c + 1) * HD)
                    for c0 in range(0, S, CW):
                        mm = split_matmul(pe, ps_s[:, c, c0:c0 + CW], (q_hi[rows, b, :], q_lo[rows, b, :]), (k_hi[rows, c0:c0 + CW], k_lo[rows, c0:c0 + CW]))
                    mm.then_inc(scored, 1)

                def step(h, t, n, on):
                    b = t % 2
                    if on(0):
                        pe.wait_ge(k_split, h + 1)
                        pe.wait_ge(q_lo_done, n + 1)
                        scores(b, n, 0, on(1))
                    if on(2):
                        pe.wait_ge(combined, n - 1)
                        if on(3):
                            pe.wait_ge(at_done, n - 2)
                        for k in range(KB):
                            mm = pe.transpose(ps_t[:, k, :], e[:, b, 0, k * P:(k + 1) * P], io["ident"][:])
                        mm.then_inc(turned, 1)
                    if on(0):
                        scores(b, n, 1, on(1))
                    if on(2):
                        hb, tb = back(h, t, 2)
                        if isinstance(n, int) and n == 2:
                            pe.wait_ge(v_loaded, 16 * KB)
                        pe.wait_ge(at_done, n - 1)
                        if on(4):
                            pe.wait_ge(stored, n - 3)
                        for k in range(KB):
                            mm = pe.matmul(ps_o[:, tb % 2, 0:P], at[:, k, :], v[:, hb, k, :] if isinstance(hb, int) else v[:, bass.ds(hb, 1), k, :].squeeze(1),
                                           start=k == 0, stop=k == KB - 1)
                        mm.then_inc(valued, 1)
                steps(pe, step)


def stage_window(nc, sem, layer, io):
    NB = TILES + 3
    W3 = 3 * P
    N = TILES * SW_KV
    with ExitStack() as ctx:
        def sb(name, shape, dt=F32):
            return ctx.enter_context(nc.sbuf_tensor("w_" + name, shape, dt))

        def sem_(name):
            return sem("w_" + name)

        k_raw = sb("k_raw", [HD, SW_KV, NB, P])
        k_hi, k_lo = sb("k_hi", [HD, SW_KV, NB, P], F32R), sb("k_lo", [HD, SW_KV, NB, P], F32R)
        v = sb("v", [P, NB, P])
        q_raw = sb("q_raw", [HD, 2, GROUP, P])
        q_hi, q_lo = sb("q_hi", [HD, 2, GROUP, P], F32R), sb("q_lo", [HD, 2, GROUP, P], F32R)
        masks = sb("masks", [P, 2, TILES, P], BF16)
        identb = sb("identb", [P, P], BF16)
        KEYS = (slice(0, 4), slice(4, NB))
        WK = 2
        WN = KD // WK
        w_raw = sb("w_raw", [P, 2, WK, D])
        w_hi, w_lo = io["w_out_hi"], io["w_out_lo"]
        e = sb("e", [P, 2, GROUP, W3])
        at = sb("at", [P, 3, GROUP, P])
        sink, neg_sink = sb("sink", [P, 8]), sb("neg_sink", [P, 8])
        st = sb("st", [P, 2, 32])
        ps_s = ctx.enter_context(nc.psum_tensor("w_ps_s", [P, GROUP, BANK], F32))
        ps_t = ctx.enter_context(nc.psum_tensor("w_ps_t", [P, 3, GROUP, P], F32))
        ps_o = ctx.enter_context(nc.psum_tensor("w_ps_o", [P, GROUP, HD], F32))

        const_loaded, keys_loaded, keys_zeroed = sem_("const_loaded"), sem_("keys_loaded"), sem_("keys_zeroed")
        k_hi_done, k_split = sem_("k_hi_done"), sem_("k_split")
        sink_loaded, sink_done = sem_("sink_loaded"), sem_("sink_done")
        w_loaded = [sem_("w_loaded0"), sem_("w_loaded1")]
        w_hi_done, w_lo_done = sem_("w_hi_done"), sem_("w_lo_done")
        q_loaded = [sem_("q_loaded0"), sem_("q_loaded1")]
        q_hi_done, q_lo_done, scored, max_done = (sem_(n) for n in ("q_hi_done", "q_lo_done", "scored", "max_done"))
        exp_done, sink_exped, inv_done, turned = (sem_(n) for n in ("exp_done", "sink_exped", "inv_done", "turned"))
        at_done, valued, stored = sem_("at_done"), sem_("valued"), sem_("stored")
        max_chain, inv_chain = sem_("max_chain"), sem_("inv_chain")

        def first_block(t):
            return t if not isinstance(t, int) or t < 8 else t + 1

        def steps(eng, step):
            for t in range(2):
                for n in range(2):
                    step(t, n, 2 * t + n, lambda k, u=2 * t + n: u - k >= 0)
            with eng.Fori(2, 8) as t:
                for n in range(2):
                    step(t, n, t * 2 + n, lambda k: True)
            for u in range(16, N + 3):
                step(u // 2, u % 2, u, lambda k, u=u: u - k < N)

        with nc.Block() as block:
            @block.gpsimd
            def _(pool):
                for blk in (0, 9, NB - 1):
                    nc.gpsimd.memset(k_raw[:, :, blk, :], 0.0)
                    last = nc.gpsimd.memset(v[:, blk, :], 0.0)
                last.then_inc(keys_zeroed, 1)

            @block.sync
            def _(sp):
                for lo, n, r0 in ((1, 8, 0), (10, 2, PROMPT)):
                    sp.dma_start(k_raw[:, :, lo:lo + n, :].rearrange("d h b t -> d h (b t)"),
                                 io["qkT"][12, :, r0:r0 + n * P].rearrange("(h d) t -> d h t", d=HD)).then_inc(keys_loaded, 16)
                    sp.dma_start(v[:, lo:lo + n, :], io["v"][r0:r0 + n * P, 512:640].rearrange("(b p) d -> p b d", p=P)).then_inc(keys_loaded, 16)

                sp.dma_start(sink[:], io["sink_b"][bass.ds(layer, 1), :].squeeze(0).partition_broadcast(P)).then_inc(sink_loaded, 16)
                sp.dma_start(identb[:], io["identb"]).then_inc(const_loaded, 16)
                sp.dma_start(masks[:], io["masks"].rearrange("s t q k -> q s t k")).then_inc(const_loaded, 16)

                def step(t, n, u, on):
                    if on(0):
                        if warm(u):
                            sp.wait_ge(q_lo_done, u - 1)
                        r0 = t * P
                        sp.dma_start(q_raw[:, n], io["qkT"][8 + 2 * n:10 + 2 * n, :, bass.ds(r0, P)].rearrange("c (g d) t -> d (c g) t", d=HD)).then_inc(q_loaded[n], 16)
                    for m in ((0, 1) if isinstance(u, int) and u == 3 else (u - 16,) if isinstance(u, int) and 18 <= u < 16 + WN else ()):
                        if m >= 2:
                            sp.wait_ge(w_lo_done, m - 1)
                        sp.dma_start(w_raw[:, m % 2], io["w_out"][bass.ds(layer, 1), m * WK * P:(m + 1) * WK * P, :].squeeze(0).rearrange("(k p) n -> p k n", p=P)).then_inc(w_loaded[m % 2], 16)
                steps(sp, step)

            @block.scalar
            def _(act):
                act.wait_ge(keys_zeroed, 1)
                act.wait_ge(keys_loaded, 64)

                def split_k(blocks):
                    act.activation(k_hi[:, :, blocks, :], k_raw[:, :, blocks, :], ACT.Copy).then_inc(k_hi_done, 1)

                split_k(KEYS[0])

                def split_q(t, n, u):
                    act.wait_ge(q_loaded[n], t * 16 + 16)
                    if warm(u):
                        act.wait_ge(scored, u * 2 - 2)
                    act.activation(q_hi[:, n], q_raw[:, n], ACT.Copy).then_inc(q_hi_done, 1)

                split_q(0, 0, 0)

                def step(t, n, u, on):
                    if on(-1):
                        split_q(t + n, 1 - n, u + 1)
                    if on(0):
                        for c in range(2):
                            act.wait_ge(max_done, u * 2 + c + 1)
                            if warm(u) and c == 0:
                                act.wait_ge(turned, u - 1)
                                act.wait_ge(inv_done, u - 1)
                            for g in (2 * c, 2 * c + 1):
                                ex = act.activation(e[:, n, g, :], ps_s[:, g, 0:W3], ACT.Exp, bias=st[:, n, 4 + g:5 + g], scale=SCALE, accum_out=st[:, n, 8 + g:9 + g])
                            ex.then_inc(exp_done, 1)
                        act.activation(st[:, n, 16:20], st[:, n, 12:16], ACT.Exp).then_inc(sink_exped, 1)
                    if on(1):
                        act.wait_ge(turned, u)
                        act.activation(at[:], ps_t[:], ACT.Copy).then_inc(at_done, 1)
                    if isinstance(u, int) and u == 0:
                        split_k(KEYS[1])
                    if isinstance(u, int) and 16 <= u < 16 + WN:
                        m = u - 16
                        act.wait_ge(w_loaded[m % 2], 16 * (m // 2 + 1))
                        act.activation(w_hi[:, m * WK:(m + 1) * WK, :], w_raw[:, m % 2], ACT.Copy).then_inc(w_hi_done, 1)
                steps(act, step)

            @block.vector
            def _(dve):
                def split_k(part):
                    dve.wait_ge(k_hi_done, part + 1)
                    blocks = KEYS[part]
                    dve.tensor_tensor(k_lo[:, :, blocks, :], k_raw[:, :, blocks, :], k_hi[:, :, blocks, :].bitcast(F32), ALU.subtract).then_inc(k_split, 1)

                split_k(0)
                dve.wait_ge(sink_loaded, 16)
                dve.tensor_scalar(neg_sink[:], sink[:], -1.0, None, ALU.mult).then_inc(sink_done, 1)
                dve.wait_ge(sink_done, 1)

                def split_q(n, u):
                    dve.wait_ge(q_hi_done, u + 1)
                    dve.tensor_tensor(q_lo[:, n], q_raw[:, n], q_hi[:, n].bitcast(F32), ALU.subtract).then_inc(q_lo_done, 1)

                split_q(0, 0)

                def maximum(n, u, c):
                    g, k = slice(2 * c, 2 * c + 2), slice(n * 4 + 2 * c, n * 4 + 2 * c + 2)
                    dve.wait_ge(scored, u * 2 + c + 1)
                    ch = Chain(dve, max_chain, u * 2 + c, 2)
                    ch.link(dve.tensor_reduce(st[:, n, 2 * c:2 * c + 2], ps_s[:, g, 0:W3], AX_X, ALU.max))
                    ch.link(dve.scalar_tensor_tensor(st[:, n, 4 + 2 * c:6 + 2 * c], st[:, n, 2 * c:2 * c + 2], -SCALE, neg_sink[:, k], ALU.mult, ALU.min))
                    ch.close()
                    dve.tensor_tensor(st[:, n, 12 + 2 * c:14 + 2 * c], st[:, n, 4 + 2 * c:6 + 2 * c], sink[:, k], ALU.add).then_inc(max_done, 1)

                def step(t, n, u, on):
                    if on(3):
                        n3 = 1 - n
                        t3 = t - 1 if n == 1 else t - 2
                        dve.wait_ge(valued, u - 2)
                        dve.tensor_tensor(io["mix"][:, bass.ds(t3, 1), 512 + n3 * 256:768 + n3 * 256].rearrange("p a (g d) -> p (a g) d", g=GROUP), ps_o[:],
                                          along(st[:, n3, 24:28], HD), ALU.mult).then_inc(stored, 1)
                    if on(0):
                        maximum(n, u, 0)
                    if on(1):
                        n1 = 1 - n
                        dve.wait_ge(sink_exped, u)
                        ch = Chain(dve, inv_chain, u - 1, 1)
                        ch.link(dve.tensor_tensor(st[:, n1, 20:24], st[:, n1, 8:12], st[:, n1, 16:20], ALU.add))
                        ch.close()
                        dve.reciprocal(st[:, n1, 24:28], st[:, n1, 20:24]).then_inc(inv_done, 1)
                    if on(0):
                        maximum(n, u, 1)
                    if on(-1):
                        split_q(1 - n, u + 1)
                    if isinstance(u, int) and u == 0:
                        split_k(1)
                    if isinstance(u, int) and 17 <= u < 17 + WN:
                        m = u - 17
                        dve.wait_ge(w_hi_done, m + 1)
                        dve.tensor_tensor(w_lo[:, m * WK:(m + 1) * WK, :], w_raw[:, m % 2], w_hi[:, m * WK:(m + 1) * WK, :].bitcast(F32), ALU.subtract).then_inc(w_lo_done, 1)
                steps(dve, step)

            @block.tensor
            def _(pe):
                pe.wait_ge(const_loaded, 32)
                pe.wait_ge(k_split, 1)

                def step(t, n, u, on):
                    if on(0):
                        if isinstance(u, int) and u == 2:
                            pe.wait_ge(k_split, 2)
                        pe.wait_ge(q_lo_done, u + 1)
                        kb = first_block(t)
                        kh, kl = (k[:, n, bass.ds(kb, 3), :].rearrange("d b t -> d (b t)") for k in (k_hi, k_lo))
                        for g in range(GROUP):
                            if on(1) and g % 2 == 0:
                                pe.wait_ge(exp_done, u * 2 - 1 + g // 2)
                                pe.sem_inc(io["held"], 1)
                            out = ps_s[:, g, 0:W3]
                            pe.matmul(out, q_hi[:, n, g, :], kh, start=True, stop=False)
                            pe.matmul(out, q_hi[:, n, g, :], kl, start=False, stop=False)
                            for side, c0 in ((0, 0), (1, 2 * P)):
                                pe.matmul(ps_s[:, g, c0:c0 + P], identb[:], masks[:, side, t, :] if isinstance(t, int) else masks[:, side, bass.ds(t, 1), :].squeeze(1),
                                          start=False, stop=False, skip_group_check=True)
                            mm = pe.matmul(out, q_lo[:, n, g, :], kh, start=False, stop=True)
                            if g % 2:
                                mm.then_inc(scored, 1)
                    if on(2):
                        t2 = t - 1
                        pe.wait_ge(at_done, u - 1)
                        if on(3):
                            pe.wait_ge(stored, u - 2)
                        fb = first_block(t2)
                        for g in range(GROUP):
                            for k in range(3):
                                mm = pe.matmul(ps_o[:, g, :], at[:, k, g, :], v[:, bass.ds(fb + k, 1), n * HD:(n + 1) * HD].squeeze(1), start=k == 0, stop=k == 2)
                        mm.then_inc(valued, 1)
                    if on(1):
                        pe.wait_ge(exp_done, u * 2)
                        if on(2):
                            pe.wait_ge(at_done, u - 1)
                        for k in range(3):
                            for g in range(GROUP):
                                mm = pe.transpose(ps_t[:, k, g, :], e[:, 1 - n, g, k * P:(k + 1) * P], io["ident"][:])
                        mm.then_inc(turned, 1)
                steps(pe, step)


def stage_mix(nc, sem, layer, io):
    with ExitStack() as ctx:
        def sb(name, shape, dt=F32):
            return ctx.enter_context(nc.sbuf_tensor("m_" + name, shape, dt))

        def sem_(name):
            return sem("m_" + name)

        w_hi, w_lo = io["w_out_hi"], io["w_out_lo"]
        router = sb("router", [P, KD, E])
        gain_h = sb("gain_h", [P, D])
        subln = sb("subln", [P, P])
        subg = sb("subg", [P, P])
        mixn = sb("mixn", [P, D])
        sq = sb("sq", [P, 512])
        mt_hi, mt_lo = sb("mt_hi", [P, 2, KD, P], F32R), sb("mt_lo", [P, 2, KD, P], F32R)
        ht = sb("ht", [P, KD, P])
        x = sb("x", [P, 2, D])
        h = sb("h", [P, 2, D])
        st = sb("st", [P, 48])
        ps_m = ctx.enter_context(nc.psum_tensor("m_ps_m", [P, KD, P], F32))
        ps_h = ctx.enter_context(nc.psum_tensor("m_ps_h", [P, KD, P], F32))
        ps_o = ctx.enter_context(nc.psum_tensor("m_ps_o", [P, D], F32))
        ps_r = ctx.enter_context(nc.psum_tensor("m_ps_r", [P, BANK], F32))

        subln_loaded, gain_loaded, router_loaded = (sem_(n) for n in ("subln_loaded", "gain_loaded", "router_loaded"))
        subg_done = sem_("subg_done")
        x_loaded = [sem_("x_loaded0"), sem_("x_loaded1")]
        x_stored = [sem_("x_stored0"), sem_("x_stored1")]
        h_stored = [sem_("h_stored0"), sem_("h_stored1")]
        squared, summed, rooted, mix_ready = (sem_(n) for n in ("squared", "summed", "rooted", "mix_ready"))
        mix_turned, mt_hi_done, mt_lo_done, mixed = (sem_(n) for n in ("mix_turned", "mt_hi_done", "mt_lo_done", "mixed"))
        x_done, x_squared, x_rooted, h_done = (sem_(n) for n in ("x_done", "x_squared", "x_rooted", "h_done"))
        h_turned, ht_done, routed, logits_done = (sem_(n) for n in ("h_turned", "ht_done", "routed", "logits_done"))
        sub_chain, h_chain = sem_("sub_chain"), sem_("h_chain")

        with nc.Block() as block:
            @block.sync
            def _(sp):
                sp.dma_start(subln[:], io["subln_a"][bass.ds(layer, 1), :].squeeze(0).partition_broadcast(P)).then_inc(subln_loaded, 16)
                sp.dma_start(gain_h[:], io["ffn_norm"][bass.ds(layer, 1), :].squeeze(0).partition_broadcast(P)).then_inc(gain_loaded, 16)
                sp.dma_start(router[:], io["w_router"][bass.ds(layer, 1)].squeeze(0).rearrange("(k p) e -> p k e", p=P)).then_inc(router_loaded, 16)

                def step(i, b, on, j):
                    if on(1):
                        if on(3):
                            sp.wait_ge(x_stored[1 - b], 16 * (j - 1 + b))
                            sp.wait_ge(h_done, i - 2)
                        sp.dma_start(x[:, 1 - b, :], io["y"][bass.ds((i - 1) * P, P), :]).then_inc(x_loaded[1 - b], 16)
                    if on(2):
                        sp.wait_ge(x_done, i * 2 - 2)
                        sp.dma_start(io["y"][bass.ds((i - 2) * P, P), :], x[:, b, :]).then_inc(x_stored[b], 16)
                        sp.wait_ge(h_done, i - 1)
                        sp.dma_start(io["h"][bass.ds((i - 2) * P, P), :], h[:, b, :]).then_inc(h_stored[b], 16)
                paired(sp, TILES, 2, step)
                for s in x_stored + h_stored:
                    sp.wait_ge(s, 16 * TILES // 2)

            @block.scalar
            def _(act):
                def step(i, b, on, j):
                    if on(1):
                        act.wait_ge(mix_turned, i)
                        if on(3):
                            act.wait_ge(mixed, i * 2 - 4)
                        act.activation(mt_hi[:, 1 - b], ps_m[:], ACT.Copy).then_inc(mt_hi_done, 1)
                    if on(0):
                        act.wait_ge(summed, i)
                        act.activation(sq[:], io["mix"][:, bass.ds(i, 1), 0:512].squeeze(1), ACT.Square).then_inc(squared, 1)
                        act.wait_ge(summed, i + 1)
                        act.activation(st[:, 4:8], st[:, 0:4], ACT.Sqrt, bias=io["eps"][:, 0:1], scale=1.0 / P).then_inc(rooted, 1)
                    if on(2):
                        act.wait_ge(x_done, i * 2 - 2)
                        if on(4):
                            act.wait_ge(h_stored[b], 16 * (j - 1))
                            act.wait_ge(h_turned, i - 3)
                        act.activation(h[:, b, :], x[:, b, :], ACT.Square, accum_out=st[:, 16 + b:17 + b]).then_inc(x_squared, 1)
                        act.wait_ge(x_squared, i - 1)
                        act.activation(st[:, 18 + b:19 + b], st[:, 16 + b:17 + b], ACT.Sqrt, bias=io["eps"][:, 0:1], scale=1.0 / D).then_inc(x_rooted, 1)
                    if on(3):
                        act.wait_ge(h_turned, i - 2)
                        if on(4):
                            act.wait_ge(routed, i - 3)
                        act.activation(ht[:], ps_h[:], ACT.Copy).then_inc(ht_done, 1)
                paired(act, TILES, 3, step)

            @block.vector
            def _(dve):
                nc.vector.engine_nop().then_inc(logits_done, 1)
                dve.wait_ge(subln_loaded, 16)
                dve.tensor_scalar(subg[:], subln[:], io["lam_rest"][:, bass.ds(layer, 1)], None, ALU.mult).then_inc(subg_done, 1)
                dve.wait_ge(subg_done, 1)

                def step(i, b, on, j):
                    if on(1):
                        dve.wait_ge(mt_hi_done, i)
                        dve.tensor_tensor(mt_lo[:, 1 - b], ps_m[:], mt_hi[:, 1 - b].bitcast(F32), ALU.subtract).then_inc(mt_lo_done, 1)
                    if on(0):
                        mix = io["mix"][:, bass.ds(i, 1), :].squeeze(1)
                        mh = mixn[:, 0:512].rearrange("p (h d) -> p h d", d=P)
                        ch = Chain(dve, sub_chain, i, 2)
                        dve.wait_ge(squared, i + 1)
                        dve.tensor_reduce(st[:, 0:4], sq[:].rearrange("p (h d) -> p h d", d=P), AX_X, ALU.add).then_inc(summed, 1)
                        dve.wait_ge(rooted, i + 1)
                        ch.link(dve.reciprocal(st[:, 8:12], st[:, 4:8]))
                        dve.wait_ge(mix_turned, i)
                        dve.tensor_copy(mixn[:, 512:1024], mix[:, 512:1024])
                        ch.link(dve.tensor_tensor(mh, mix[:, 0:512].rearrange("p (h d) -> p h d", d=P), along(st[:, 8:12], P), ALU.mult))
                        ch.close()
                        dve.tensor_tensor(mh, mh, over(subg[:], 4), ALU.mult).then_inc(mix_ready, 1)
                    if on(2):
                        dve.wait_ge(x_loaded[b], 16 * j)
                        for half in range(2):
                            c = slice(half * BANK, (half + 1) * BANK)
                            dve.wait_ge(mixed, i * 2 - 3 + half)
                            dve.tensor_tensor(x[:, b, c], ps_o[:, c], x[:, b, c], ALU.add).then_inc(x_done, 1)
                        if isinstance(i, int) and i == 2:
                            dve.wait_ge(gain_loaded, 16)
                        dve.wait_ge(x_rooted, i - 1)
                        ch = Chain(dve, h_chain, i - 2, 1)
                        ch.link(dve.reciprocal(st[:, 20 + b:21 + b], st[:, 18 + b:19 + b]))
                        ch.close()
                        dve.scalar_tensor_tensor(h[:, b, :], x[:, b, :], st[:, 20 + b:21 + b], gain_h[:], ALU.mult, ALU.mult).then_inc(h_done, 1)
                    if on(4):
                        dve.wait_ge(routed, i - 3)
                        dve.tensor_copy(io["logits"][:, bass.ds(i - 4, 1), :].squeeze(1), ps_r[:, 0:E]).then_inc(logits_done, 1)
                paired(dve, TILES, 4, step)

            @block.tensor
            def _(pe):
                def step(i, b, on, j):
                    if on(1):
                        pe.wait_ge(mix_ready, i)
                        if on(2):
                            pe.wait_ge(mt_lo_done, i - 1)
                        for k in range(KD):
                            mm = pe.transpose(ps_m[:, k, :], mixn[:, k * P:(k + 1) * P], io["ident"][:])
                        mm.then_inc(mix_turned, 1)
                    if on(2):
                        pe.wait_ge(mt_lo_done, i - 1)
                        for half in range(2):
                            if on(3):
                                pe.wait_ge(x_done, i * 2 - 5 + half)
                            c = slice(half * BANK, (half + 1) * BANK)
                            for k in range(KD):
                                mm = split_matmul(pe, ps_o[:, c], (mt_hi[:, b, k, :], mt_lo[:, b, k, :]), (w_hi[:, k, c], w_lo[:, k, c]), k == 0, k == KD - 1)
                            mm.then_inc(mixed, 1)
                    if on(4):
                        if isinstance(i, int) and i == 4:
                            pe.wait_ge(router_loaded, 16)
                        pe.wait_ge(ht_done, i - 3)
                        pe.wait_ge(logits_done, i - 3)
                        for k in range(KD):
                            mm = pe.matmul(ps_r[:, 0:E], ht[:, k, :], router[:, k, :], start=k == 0, stop=k == KD - 1)
                        mm.then_inc(routed, 1)
                    if on(3):
                        pe.wait_ge(h_done, i - 2)
                        if on(4):
                            pe.wait_ge(ht_done, i - 3)
                        for k in range(KD):
                            mm = pe.transpose(ps_h[:, k, :], h[:, 1 - b, k * P:(k + 1) * P], io["ident"][:])
                        mm.then_inc(h_turned, 1)
                paired(pe, TILES, 4, step)


def stage_choose(nc, sem, layer, io):
    KP = PLE // P
    G = 32 + E
    R = TILES * E
    with ExitStack() as ctx:
        def sb(name, shape, dt=F32):
            return ctx.enter_context(nc.sbuf_tensor("c_" + name, shape, dt))

        def sem_(name):
            return sem("c_" + name)

        z = sb("z", [P, TILES, E])
        mx, total, inv = sb("mx", [P, TILES]), sb("total", [P, TILES]), sb("inv", [P, TILES])
        aff = sb("aff", [G, PROMPT])
        vals = sb("vals", [G, CAP_P])
        rows = sb("rows", [G, CAP_P], U32)
        rows_f = sb("rows_f", [G, CAP_P])
        ps_a = ctx.enter_context(nc.psum_tensor("c_ps_a", [E, 3, BANK], F32))
        ps_v = ctx.enter_context(nc.psum_tensor("c_ps_v", [P, BANK], F32))
        ps_i = ctx.enter_context(nc.psum_tensor("c_ps_i", [P, BANK], F32))
        p, pt = sb("p", [P, 2, PLE]), sb("pt", [P, 2, KP, P])
        wp = sb("wp", [P, KP, D])
        ps_p = ctx.enter_context(nc.psum_tensor("c_ps_p", [P, KP, P], F32))
        ps_e = ctx.enter_context(nc.psum_tensor("c_ps_e", [P, 2, BANK], F32))
        wp_loaded, p_turned, pt_done, embed_mm, embed_done = (sem_(n) for n in ("wp_loaded", "p_turned", "pt_done", "embed_mm", "embed_done"))
        p_loaded = [sem_("p_loaded0"), sem_("p_loaded1")]
        soft_chain, shifted, exp_done, soft_done, cleared = (sem_(n) for n in ("soft_chain", "shifted", "exp_done", "soft_done", "cleared"))
        turned, aff_ready, top_chain, lists_ready, lists_turned = (sem_(n) for n in ("turned", "aff_ready", "top_chain", "lists_ready", "lists_turned"))
        tables_done, listed = sem_("tables_done"), sem_("listed")

        with nc.Block() as block:
            @block.sync
            def _(sp):
                sp.dma_start(wp[:], io["w_ple_proj"][bass.ds(layer, 1)].squeeze(0).rearrange("(k p) n -> p k n", p=P)).then_inc(wp_loaded, 16)

                def step(i, b, on, j):
                    if on(2):
                        sp.wait_ge(p_turned, i - 1)
                    sp.dma_start(p[:, b, :], io["p"][bass.ds(layer * ROWS + i * P, P), :]).then_inc(p_loaded[b], 16)
                paired(sp, TILES, 0, step)

            @block.scalar
            def _(act):
                act.wait_ge(shifted, 1)
                act.activation(z[:], z[:], ACT.Exp).then_inc(exp_done, 1)
                act.wait_ge(cleared, 1)
                act.wait_ge(turned, 1)
                act.activation(aff[0:E, :].rearrange("e (a t) -> e a t", a=2), ps_a[:, 0:2, :], ACT.Copy).then_inc(aff_ready, 1)
                act.activation(aff[32:32 + E, 0:SAMPLE], ps_a[:, 2, 0:SAMPLE], ACT.Copy).then_inc(aff_ready, 1)

                def step(i, b, on, j):
                    if on(0):
                        act.wait_ge(p_turned, i + 1)
                        if on(2):
                            act.wait_ge(embed_mm, i * 2 - 2)
                        act.activation(pt[:, b], ps_p[:], ACT.Copy).then_inc(pt_done, 1)
                    if on(1):
                        for c in range(2):
                            act.wait_ge(embed_mm, i * 2 - 1 + c)
                            act.activation(io["mix"][:, bass.ds(i - 1, 1), c * BANK:(c + 1) * BANK].squeeze(1), ps_e[:, c, :], ACT.Copy).then_inc(embed_done, 1)
                paired(act, TILES, 1, step)

            @block.gpsimd
            def _(pool):
                nc.gpsimd.memset(aff[:], -1.0).then_inc(cleared, 1)

            @block.tensor
            def _(pe):
                pe.wait_ge(soft_done, 1)
                for t in range(TILES):
                    mm = pe.transpose(ps_a[:, t // 4, (t % 4) * P:(t % 4 + 1) * P], z[:, t, :], io["ident"][:])
                mm.then_inc(turned, 1)

                def step(i, b, on, j):
                    if on(0):
                        pe.wait_ge(p_loaded[b], j * 16 + 16)
                        if on(1):
                            pe.wait_ge(pt_done, i)
                        for k in range(KP):
                            mm = pe.transpose(ps_p[:, k, :], p[:, b, k * P:(k + 1) * P], io["ident"][:])
                        mm.then_inc(p_turned, 1)
                    if on(1):
                        if isinstance(i, int) and i == 1:
                            pe.wait_ge(wp_loaded, 16)
                        pe.wait_ge(pt_done, i)
                        for c in range(2):
                            if on(2):
                                pe.wait_ge(embed_done, i * 2 - 3 + c)
                            for k in range(KP):
                                mm = pe.matmul(ps_e[:, c, :], pt[:, 1 - b, k, :], wp[:, k, c * BANK:(c + 1) * BANK], start=k == 0, stop=k == KP - 1)
                            mm.then_inc(embed_mm, 1)
                paired(pe, TILES, 1, step)
                pe.wait_ge(lists_ready, 1)
                pe.transpose(ps_v[:, 0:G], vals[:], io["ident"][0:G, 0:G])
                pe.transpose(ps_i[:, 0:G], rows_f[:], io["ident"][0:G, 0:G]).then_inc(lists_turned, 1)

            @block.vector
            def _(dve):
                ch = Chain(dve, soft_chain, 0, 3)
                ch.link(dve.tensor_reduce(mx[:], io["logits"][:], AX_X, ALU.max))
                dve.tensor_tensor(z[:], io["logits"][:], along(mx[:], E), ALU.subtract).then_inc(shifted, 1)
                dve.wait_ge(exp_done, 1)
                ch.link(dve.tensor_reduce(total[:], z[:], AX_X, ALU.add))
                ch.link(dve.reciprocal(inv[:], total[:]))
                ch.close()
                dve.tensor_tensor(z[:], z[:], along(inv[:], E), ALU.mult).then_inc(soft_done, 1)
                dve.wait_ge(aff_ready, 2)
                rounds = CAP_P // 8
                ch = Chain(dve, top_chain, 0, 2 * rounds)
                for r in range(rounds):
                    c = slice(8 * r, 8 * r + 8)
                    ch.link(dve.max(vals[:, c], aff[:]))
                    dve.max_index(rows[:, c], vals[:, c], aff[:])
                    if r < rounds - 1:
                        ch.link(dve.match_replace(aff[:], vals[:, c], aff[:], -2.0))
                nc.vector.engine_nop().then_inc(listed, 1)
                dve.wait_ge(listed, 1)
                ch.link(dve.tensor_copy(rows_f[:], rows[:]))
                ch.close()
                nc.vector.engine_nop().then_inc(lists_ready, 1)
                dve.wait_ge(lists_turned, 1)
                dve.tensor_copy(io["vals"][:, 0, :], ps_v[:, 0:E])
                dve.tensor_copy(io["vals"][:, 1, :], ps_v[:, 32:G])
                dve.tensor_copy(io["rows"][:, 0, :], ps_i[:, 0:E])
                dve.tensor_scalar(io["rows"][:, 1, :], ps_i[:, 32:G], float(PROMPT), None, ALU.add).then_inc(tables_done, 1)


def stage_experts(nc, sem, layer, io):
    NS, CH = 12, 256
    RING = 4
    GK, GN = 2, KD // 2
    B2 = CH // P
    with ExitStack() as ctx:
        def sb(name, shape, dt=F32):
            return ctx.enter_context(nc.sbuf_tensor("e_" + name, shape, dt))

        def sem_(name):
            return sem("e_" + name)

        w = sb("w", [P, RING, KD, CH])
        xp, xs = sb("xp", [P, D]), sb("xs", [CAP_S, D])
        g_raw = sb("g_raw", [P, 2, GK, D])
        g_hi, g_lo = io["w_ple_hi"], io["w_ple_lo"]
        xt = sb("xt", [P, KD, SLOTS])
        gate = sb("gate", [P, B2, SLOTS])
        hid = sb("hid", [P, KD, SLOTS])
        yt = sb("yt", [P, 2, B2, SLOTS])
        yp, ys = sb("yp", [P, D]), sb("ys", [CAP_S, D])
        ip_g, is_g, ip_s, is_s = (sb(n, [P, 1], U32) for n in ("ip_g", "is_g", "ip_s", "is_s"))
        ps_w = ctx.enter_context(nc.psum_tensor("e_ps_w", [P, 4, BANK], F32))
        ps_x = ctx.enter_context(nc.psum_tensor("e_ps_x", [P, 2, BANK], F32))
        ps_y = ctx.enter_context(nc.psum_tensor("e_ps_y", [P, 2, BANK], F32))

        w_loaded = [sem_(f"w_loaded{r}") for r in range(RING)]
        g_loaded = [sem_("g_loaded0"), sem_("g_loaded1")]
        g_hi_done, g_lo_done = sem_("g_hi_done"), sem_("g_lo_done")
        piece_done = sem_("piece_done")
        g_rows, s_rows = sem_("g_rows"), sem_("s_rows")
        gathered, scattered, held = io["gathered"], io["scattered"], io["held"]
        x_turned, xt_done = sem_("x_turned"), sem_("xt_done")
        silu_done, hid_done = sem_("silu_done"), sem_("hid_done")
        yt_done, y_turned, y_done = sem_("yt_done"), sem_("y_turned"), sem_("y_done")

        def source(e, s):
            name, q = (("w_gate_e", "w_up_e")[s % 2], s // 2) if s < 8 else ("w_down_e", s - 8)
            return io[name][bass.ds(layer * E + e, 1), :, q * CH:(q + 1) * CH].squeeze(0).rearrange("(k p) f -> p k f", p=P)

        def experts(eng, body):
            body(0, True, True)
            with eng.Fori(1, E - 1) as e:
                body(e, False, True)
            body(E - 1, False, False)

        with nc.Block() as block:
            @block.sync
            def _(sp):
                for s in range(RING):
                    if s == RING // 2:
                        sp.wait_ge(x_turned, 1)
                    sp.dma_start(w[:, s], source(0, s)).then_inc(w_loaded[s], 16)

                def body(e, first, more):
                    for s in range(NS):
                        if s + RING < NS or more:
                            sp.wait_ge(piece_done, e * NS + s + 1)
                            sp.sem_inc(held, 1)
                            sp.dma_start(w[:, s % RING], source(e, s + RING) if s + RING < NS else source(e + 1, s + RING - NS)).then_inc(w_loaded[s % RING], 16)
                        if first and s % 2 and s // 2 < GN:
                            n = s // 2
                            if n >= 2:
                                sp.wait_ge(g_lo_done, n - 1)
                            sp.dma_start(g_raw[:, n % 2], io["w_ple_gate"][bass.ds(layer, 1), n * GK * P:(n + 1) * GK * P, :].squeeze(0).rearrange("(k p) n -> p k n", p=P)).then_inc(g_loaded[n % 2], 16)
                experts(sp, body)

            @block.gpsimd
            def _(pool):
                def gather(e):
                    pool.wait_ge(x_turned, e * 4)
                    pool.sem_inc(held, 1)
                    nc.gpsimd.tensor_copy(ip_g[:], io["rows"][:, 0, bass.ds(e, 1)])
                    nc.gpsimd.tensor_copy(is_g[0:CAP_S], io["rows"][0:CAP_S, 1, bass.ds(e, 1)]).then_inc(g_rows, 1)
                    pool.wait_ge(g_rows, e + 1)
                    pool.sem_inc(held, 1)
                    nc.gpsimd.indirect_dma_start(xp[:], None, io["h"], bass.IndirectOffsetOnAxis(ap=ip_g[:, 0:1], axis=0)).then_inc(gathered, 16)
                    nc.gpsimd.indirect_dma_start(xs[:], None, io["h"], bass.IndirectOffsetOnAxis(ap=is_g[0:CAP_S, 0:1], axis=0)).then_inc(gathered, 16)

                def scatter(e, first):
                    if not first:
                        pool.wait_ge(scattered, (layer * E + e) * 32)
                        pool.sem_inc(held, 1)
                    nc.gpsimd.tensor_copy(ip_s[:], io["rows"][:, 0, bass.ds(e, 1)])
                    nc.gpsimd.tensor_copy(is_s[0:CAP_S], io["rows"][0:CAP_S, 1, bass.ds(e, 1)]).then_inc(s_rows, 1)
                    pool.wait_ge(s_rows, e + 1)
                    pool.wait_ge(y_done, e * 4 + 4)
                    pool.sem_inc(held, 1)
                    nc.gpsimd.indirect_dma_start(io["y"], bass.IndirectOffsetOnAxis(ap=ip_s[:, 0:1], axis=0), yp[:], None, compute_op=ALU.add).then_inc(scattered, 16)
                    nc.gpsimd.indirect_dma_start(io["y"], bass.IndirectOffsetOnAxis(ap=is_s[0:CAP_S, 0:1], axis=0), ys[:], None, compute_op=ALU.add).then_inc(scattered, 16)

                gather(0)

                def body(e, first, more):
                    if more:
                        gather(e + 1)
                    scatter(e, first)
                experts(pool, body)
                pool.wait_ge(scattered, (layer + 1) * E * 32)
                pool.sem_inc(held, 1)

            @block.scalar
            def _(act):
                def x_part(e, g):
                    act.wait_ge(x_turned, e * 4 + g + 1)
                    act.activation(xt[:, 2 * g:2 * g + 2, :], ps_x[:, g % 2, 0:B2 * SLOTS].rearrange("p (k t) -> p k t", k=B2), ACT.Copy).then_inc(xt_done, 1)

                def split(n):
                    act.wait_ge(g_loaded[n % 2], 16 * (n // 2 + 1))
                    act.activation(g_hi[:, n * GK:(n + 1) * GK, :], g_raw[:, n % 2], ACT.Copy).then_inc(g_hi_done, 1)

                for g in range(4):
                    x_part(0, g)

                def body(e, first, more):
                    for s in range(NS):
                        out = ps_w[:, s % 4, 0:B2 * SLOTS].rearrange("p (k t) -> p k t", k=B2)
                        if s < 8 and s % 2 == 0:
                            act.wait_ge(piece_done, e * NS + s + 1)
                            act.wait_ge(hid_done, e * 4 + s // 2)
                            act.activation(gate[:], out, ACT.Silu).then_inc(silu_done, 1)
                        if s >= 8:
                            q = s - 8
                            act.wait_ge(piece_done, e * NS + s + 1)
                            if not first or q > 1:
                                act.wait_ge(y_turned, e * 4 + q - 1)
                            act.activation(yt[:, q % 2], out, ACT.Copy).then_inc(yt_done, 1)
                            if more and q < 2:
                                x_part(e + 1, 2 * q)
                                x_part(e + 1, 2 * q + 1)
                        if first and s % 2 and 1 <= s // 2 <= GN:
                            split(s // 2 - 1)
                experts(act, body)

            @block.vector
            def _(dve):
                def y_part(e, q):
                    c = slice(q * CH, (q + 1) * CH)
                    dve.wait_ge(y_turned, e * 4 + q + 1)
                    if q == 0 and not (isinstance(e, int) and e == 0):
                        dve.wait_ge(scattered, (layer * E + e) * 32)
                    dve.tensor_scalar(yp[:, c], ps_y[:, q % 2, 0:CH], io["vals"][:, 0, bass.ds(e, 1)], None, ALU.mult)
                    dve.tensor_scalar(ys[:, c], ps_y[0:CAP_S, q % 2, CH:2 * CH], io["vals"][0:CAP_S, 1, bass.ds(e, 1)], None, ALU.mult).then_inc(y_done, 1)

                def split(n):
                    dve.wait_ge(g_hi_done, n + 1)
                    dve.tensor_tensor(g_lo[:, n * GK:(n + 1) * GK, :], g_raw[:, n % 2], g_hi[:, n * GK:(n + 1) * GK, :].bitcast(F32), ALU.subtract).then_inc(g_lo_done, 1)

                def body(e, first, more):
                    if not first:
                        y_part(e - 1, 3)
                    for q in range(4):
                        dve.wait_ge(piece_done, e * NS + 2 * q + 2)
                        dve.wait_ge(silu_done, e * 4 + q + 1)
                        dve.tensor_tensor(hid[:, 2 * q:2 * q + 2, :], ps_w[:, (2 * q + 1) % 4, 0:B2 * SLOTS].rearrange("p (k t) -> p k t", k=B2), gate[:], ALU.mult).then_inc(hid_done, 1)
                        if first and q:
                            split(q - 1)
                    for q in range(3):
                        y_part(e, q)
                        if first and q == 0:
                            split(3)
                experts(dve, body)
                y_part(E - 1, 3)

            @block.tensor
            def _(pe):
                def turn_x(e, g):
                    if g == 0:
                        pe.wait_ge(gathered, (layer * E + e) * 32 + 32)
                    if not isinstance(e, int) or e or g >= 2:
                        pe.wait_ge(xt_done, e * 4 + g - 1)
                    for k in range(B2):
                        c = slice((2 * g + k) * P, (2 * g + k + 1) * P)
                        pe.transpose(ps_x[:, g % 2, k * SLOTS:k * SLOTS + P], xp[:, c], io["ident"][:])
                        mm = pe.transpose(ps_x[:, g % 2, k * SLOTS + P:(k + 1) * SLOTS], xs[:, c], io["ident"][0:CAP_S, 0:CAP_S])
                    mm.then_inc(x_turned, 1)

                def turn_y(e, q):
                    pe.wait_ge(yt_done, e * 4 + q + 1)
                    if not isinstance(e, int) or e or q >= 2:
                        pe.wait_ge(y_done, e * 4 + q - 1)
                    for k in range(B2):
                        pe.transpose(ps_y[:, q % 2, k * P:(k + 1) * P], yt[:, q % 2, k, 0:P], io["ident"][:])
                        mm = pe.transpose(ps_y[0:CAP_S, q % 2, CH + k * P:CH + (k + 1) * P], yt[:, q % 2, k, P:SLOTS], io["ident"][:])
                    mm.then_inc(y_turned, 1)

                for g in range(4):
                    turn_x(0, g)

                def body(e, first, more):
                    for s in range(NS):
                        pe.wait_ge(w_loaded[s % RING], e * (16 * NS // RING) + 16 * (s // RING) + 16)
                        if s == 0:
                            pe.wait_ge(xt_done, e * 4 + 4)
                        if s >= 4:
                            pe.wait_ge(hid_done, e * 4 + s // 2 - 1)
                        elif not first:
                            pe.wait_ge(yt_done, e * 4 - 3 + s)
                        groups = ((range(0, 6), 3), (range(6, 8), 4)) if s == 8 else ((range(KD), 0),)
                        for ks, need in groups:
                            if need:
                                pe.wait_ge(hid_done, e * 4 + need)
                            for m in range(B2):
                                for k in ks:
                                    mm = pe.matmul(ps_w[:, s % 4, m * SLOTS:(m + 1) * SLOTS], w[:, s % RING, k, m * P:(m + 1) * P],
                                                   (xt if s < 8 else hid)[:, k, :], start=k == 0 and m == 0, stop=k == KD - 1, skip_group_check=True)
                        mm.then_inc(piece_done, 1)
                        if more and s in (8, 9):
                            turn_x(e + 1, 2 * (s - 8))
                            turn_x(e + 1, 2 * (s - 8) + 1)
                        if s == 0 and not first:
                            turn_y(e - 1, 3)
                        if s > 8:
                            turn_y(e, s - 9)
                experts(pe, body)
                turn_y(E - 1, 3)


def stage_embed(nc, sem, layer, io):
    with ExitStack() as ctx:
        def sb(name, shape, dt=F32):
            return ctx.enter_context(nc.sbuf_tensor("g_" + name, shape, dt))

        def sem_(name):
            return sem("g_" + name)

        w_hi, w_lo = io["w_ple_hi"], io["w_ple_lo"]
        gain = sb("gain", [P, D])
        x, xn = sb("x", [P, 2, D]), sb("xn", [P, D])
        x_res, sq = sb("x_res", [P, 2, D]), sb("sq", [P, D])
        at_hi, at_lo = sb("at_hi", [P, 2, KD, P], F32R), sb("at_lo", [P, 2, KD, P], F32R)
        gate, out = sb("gate", [P, 2, BANK]), sb("out", [P, 2, D])
        st = sb("st", [P, 16])
        ps_x = ctx.enter_context(nc.psum_tensor("g_ps_x", [P, KD, P], F32))
        ps_g = ctx.enter_context(nc.psum_tensor("g_ps_g", [P, 2, BANK], F32))

        gain_loaded = sem_("gain_loaded")
        x_loaded = [sem_("x_loaded0"), sem_("x_loaded1")]
        res_loaded = [sem_("res_loaded0"), sem_("res_loaded1")]
        y_stored = [sem_("y_stored0"), sem_("y_stored1")]
        squared, rooted, normed, turned = (sem_(n) for n in ("squared", "rooted", "normed", "turned"))
        at_hi_done, at_lo_done, gate_mm = (sem_(n) for n in ("at_hi_done", "at_lo_done", "gate_mm"))
        gated, y_done, norm_chain, out_chain = (sem_(n) for n in ("gated", "y_done", "norm_chain", "out_chain"))

        with nc.Block() as block:
            @block.sync
            def _(sp):
                def step(i, b, on, j):
                    if on(0):
                        if warm(i):
                            sp.wait_ge(normed, i - 1)
                        sp.dma_start(x[:, b, :], io["y"][bass.ds(i * P, P), :]).then_inc(x_loaded[b], 16)
                    if isinstance(i, int) and i == 0:
                        sp.dma_start(gain[:], io["ple_norm"][bass.ds(layer, 1), :].squeeze(0).partition_broadcast(P)).then_inc(gain_loaded, 16)
                    if on(1):
                        if on(3):
                            sp.wait_ge(y_done, i * 2 - 4)
                        sp.dma_start(x_res[:, 1 - b, :], io["y"][bass.ds((i - 1) * P, P), :]).then_inc(res_loaded[1 - b], 16)
                    if on(2):
                        sp.wait_ge(y_done, i * 2 - 2)
                        sp.dma_start(io["y"][bass.ds((i - 2) * P, P), :], out[:, b, :]).then_inc(y_stored[b], 16)
                paired(sp, TILES, 2, step)
                for s in y_stored:
                    sp.wait_ge(s, 16 * TILES // 2)

            @block.scalar
            def _(act):
                def step(i, b, on, j):
                    if on(1):
                        act.wait_ge(turned, i)
                        if on(3):
                            act.wait_ge(gate_mm, i * 2 - 4)
                        act.activation(at_hi[:, 1 - b], ps_x[:], ACT.Copy).then_inc(at_hi_done, 1)
                    if on(0):
                        act.wait_ge(x_loaded[b], j * 16 + 16)
                        if on(1):
                            act.wait_ge(squared, i)
                        act.activation(sq[:], x[:, b, :], ACT.Square, accum_out=st[:, b:b + 1]).then_inc(squared, 1)
                        act.wait_ge(squared, i + 1)
                        act.activation(st[:, 2 + b:3 + b], st[:, b:b + 1], ACT.Sqrt, bias=io["eps"][:, 0:1], scale=1.0 / D).then_inc(rooted, 1)
                    if on(2):
                        for c in range(2):
                            act.wait_ge(gate_mm, i * 2 - 4 + c + 1)
                            if on(3):
                                act.wait_ge(y_done, i * 2 - 4)
                            act.activation(gate[:, c, :], ps_g[:, c, :], ACT.Sigmoid).then_inc(gated, 1)
                paired(act, TILES, 2, step)

            @block.vector
            def _(dve):
                dve.wait_ge(gain_loaded, 16)

                def step(i, b, on, j):
                    if on(1):
                        dve.wait_ge(at_hi_done, i)
                        dve.tensor_tensor(at_lo[:, 1 - b], ps_x[:], at_hi[:, 1 - b].bitcast(F32), ALU.subtract).then_inc(at_lo_done, 1)
                    if on(0):
                        dve.wait_ge(rooted, i + 1)
                        ch = Chain(dve, norm_chain, i, 1)
                        ch.link(dve.reciprocal(st[:, 4 + b:5 + b], st[:, 2 + b:3 + b]))
                        ch.close()
                        dve.wait_ge(turned, i)
                        dve.scalar_tensor_tensor(xn[:], x[:, b, :], st[:, 4 + b:5 + b], gain[:], ALU.mult, ALU.mult).then_inc(normed, 1)
                    if on(2):
                        dve.wait_ge(res_loaded[b], j * 16)
                        if on(4):
                            dve.wait_ge(y_stored[b], (j - 1) * 16)
                        for c in range(2):
                            cs = slice(c * BANK, (c + 1) * BANK)
                            n = i * 2 - 4 + c
                            dve.wait_ge(gated, n + 1)
                            ch = Chain(dve, out_chain, n, 1)
                            ch.link(dve.tensor_tensor(out[:, b, cs], io["mix"][:, bass.ds(i - 2, 1), cs].squeeze(1), gate[:, c, :], ALU.mult))
                            ch.close()
                            dve.tensor_tensor(out[:, b, cs], out[:, b, cs], x_res[:, b, cs], ALU.add).then_inc(y_done, 1)
                paired(dve, TILES, 2, step)

            @block.tensor
            def _(pe):
                def step(i, b, on, j):
                    if on(1):
                        pe.wait_ge(normed, i)
                        if on(2):
                            pe.wait_ge(at_lo_done, i - 1)
                        for k in range(KD):
                            mm = pe.transpose(ps_x[:, k, :], xn[:, k * P:(k + 1) * P], io["ident"][:])
                        mm.then_inc(turned, 1)
                    if on(2):
                        pe.wait_ge(at_lo_done, i - 1)
                        for c in range(2):
                            cs = slice(c * BANK, (c + 1) * BANK)
                            if on(3):
                                pe.wait_ge(gated, i * 2 - 5 + c)
                            for k in range(KD):
                                mm = split_matmul(pe, ps_g[:, c, :], (at_hi[:, b, k, :], at_lo[:, b, k, :]), (w_hi[:, k, cs], w_lo[:, k, cs]), k == 0, k == KD - 1)
                            mm.then_inc(gate_mm, 1)
                paired(pe, TILES, 2, step)


@contextmanager
def counted(nc):
    with ExitStack() as ctx:
        sems = []

        def sem(name):
            sems.append(ctx.enter_context(nc.semaphore(name)))
            return sems[-1]

        yield sem
        numbers = sorted(s.num for s in sems)
        starts = [n for n in numbers if n - 1 not in numbers]
        ends = [n + 1 for n in numbers if n + 1 not in numbers]
        with nc.Block() as block:
            @block.sync
            def _(sp):
                for start, end in zip(starts, ends):
                    sp.sem_clear(range(start, end))


def encoder(nc, io):
    io = dict(io)
    io["w_gate_e"], io["w_up_e"], io["w_down_e"] = (io[n].rearrange("l e d f -> (l e) d f") for n in ("w_gate_e", "w_up_e", "w_down_e"))
    io["qkT"] = nc.dram_tensor("qkT", [NQK, P, ROWS], F32, kind="Internal").ap()
    io["v"] = nc.dram_tensor("v", [ROWS, V_W], F32, kind="Internal").ap()
    io["h"] = nc.dram_tensor("h", [ROWS, D], F32, kind="Internal").ap()
    with ExitStack() as ctx:
        ident = ctx.enter_context(nc.sbuf_tensor("ident", [P, P], F32))
        small = ctx.enter_context(nc.sbuf_tensor("small", [P, 8], F32))
        logits = ctx.enter_context(nc.sbuf_tensor("logits", [P, TILES, E], F32))
        vals = ctx.enter_context(nc.sbuf_tensor("vals", [P, 2, E], F32))
        rows = ctx.enter_context(nc.sbuf_tensor("rows", [P, 2, E], U32))
        start_loaded = ctx.enter_context(nc.semaphore("start_loaded"))
        own = {n: ctx.enter_context(nc.semaphore(n)) for n in ("gathered", "scattered", "held")}
        io.update(own)
        io.update(ident=ident, logits=logits, vals=vals, rows=rows, eps=small[:, 4:5], lam_init=small[:, 0:2], lam_rest=small[:, 2:4])

        with nc.Block() as block:
            @block.sync
            def _(sp):
                sp.dma_start(ident[:], io["ident_in"]).then_inc(start_loaded, 16)
                sp.dma_start(small[:], io["small_in"]).then_inc(start_loaded, 16)
                sp.dma_start(io["y"], io["x"]).then_inc(start_loaded, 16)
                sp.wait_ge(start_loaded, 48)

        with nc.Fori(0, DEPTH) as layer:
            with counted(nc) as sem:
                stage_project(nc, sem, layer, io)
            with nc.sbuf_tensor("mix", [P, TILES, D], F32) as mix:
                io["mix"] = mix
                with nc.sbuf_tensor("w_out_hi", [P, KD, D], F32R) as io["w_out_hi"], nc.sbuf_tensor("w_out_lo", [P, KD, D], F32R) as io["w_out_lo"]:
                    with counted(nc) as sem:
                        stage_dense(nc, sem, layer, io, 0, PROMPT)
                        stage_dense(nc, sem, layer, io, PROMPT, SAMPLE)
                        stage_window(nc, sem, layer, io)
                    with counted(nc) as sem:
                        stage_mix(nc, sem, layer, io)
                        stage_choose(nc, sem, layer, io)
                with nc.sbuf_tensor("w_ple_hi", [P, KD, D], F32R) as io["w_ple_hi"], nc.sbuf_tensor("w_ple_lo", [P, KD, D], F32R) as io["w_ple_lo"], counted(nc) as sem:
                    stage_experts(nc, sem, layer, io)
                    stage_embed(nc, sem, layer, io)


def constants():
    inv = np.float32(10000.0) ** (-np.arange(0, HD, 2, dtype=np.float32) / np.float32(HD))
    pos = np.concatenate([np.arange(PROMPT), np.arange(SAMPLE)]).astype(np.float32)
    ang = pos[:, None] * inv[None, :].astype(np.float32)
    cos, sin = np.cos(ang), np.sin(ang)
    trig = np.concatenate([cos, cos, -sin, sin], axis=1).astype(np.float32)
    masks = np.zeros((2, TILES, P, P), np.float32)
    q, k = np.arange(P)[:, None], np.arange(P)[None, :]
    masks[0][:, (k < q)] = MASKED / SCALE
    masks[1][:, (k > q)] = MASKED / SCALE
    masks[0, [0, PROMPT // P]] = MASKED / SCALE
    masks[1, [PROMPT // P - 1, TILES - 1]] = MASKED / SCALE
    small = np.zeros((P, 8), np.float32)
    for i in range(DEPTH):
        lam_init = 0.8 - 0.6 * math.exp(-0.3 * i)
        small[:, i] = lam_init
        small[:, 2 + i] = 1.0 - lam_init
    small[:, 4] = EPS
    return trig, masks, small


def kernel(**inputs):
    import ml_dtypes
    import concourse.bacc as bacc
    from concourse.bass_utils import run_bass_kernel_spmd

    def rows_of(a, b):
        return np.concatenate([np.asarray(a), np.asarray(b)], axis=-2)

    trig, masks, small = constants()
    given = {n: np.ascontiguousarray(v) for n, v in inputs.items() if n not in ("x_prompt", "x_sample", "p_prompt", "p_sample")}
    given["x"] = rows_of(inputs["x_prompt"], inputs["x_sample"]).reshape(ROWS, D)
    given["p"] = rows_of(inputs["p_prompt"], inputs["p_sample"]).reshape(DEPTH * ROWS, PLE)
    given.update(trig=trig, masks=masks.astype(ml_dtypes.bfloat16), small_in=small,
                 ident_in=np.eye(P, dtype=np.float32), identb=np.eye(P, dtype=ml_dtypes.bfloat16))
    nc = bacc.Bacc("TRN2", target_bir_lowering=False, num_devices=1)
    io = {n: nc.dram_tensor(f"in_{n}", a.shape, mybir.dt.from_np(a.dtype), kind="ExternalInput").ap() for n, a in given.items()}
    io["y"] = nc.dram_tensor("y", (ROWS, D), F32, kind="ExternalOutput").ap()
    encoder(nc, io)
    r = run_bass_kernel_spmd(nc, [{f"in_{n}": a for n, a in given.items()}], core_ids=[0])
    y = r.results[0]["y"]
    return y[:PROMPT].reshape(1, PROMPT, D), y[PROMPT:].reshape(1, SAMPLE, D)
```
